# Optimizing a Trainium2 kernel written in Bass

```python
import jax
import jax.numpy as jnp
from jax import lax
import numpy as np

D_MODEL = 1024
BATCH = 1
SEQ = 512
DEPTH = 2

CTX_LEN = 256
GRID_W = 64
N_EVEN = (DEPTH + 1) // 2
N_ODD = DEPTH // 2
CONV_W = D_MODEL
CONV_K = 31
POOL_WINDOWS = (2, 4, 8, 16)
POOL_GROUPS = 4
POOL_W = D_MODEL
POOL_GC = POOL_W // POOL_GROUPS
AB_IN = 2 * CONV_W + POOL_W
AB_OUT = CONV_W + POOL_W
MLSTM_E = 2 * D_MODEL
MLSTM_H = 4
MLSTM_DH = MLSTM_E // MLSTM_H
QKV_BLOCK = 4
SHORT_K = 4
CHUNK = 64
N_EXPERTS = 16
N_GROUPS = 4
EXPERTS_PER_GROUP = N_EXPERTS // N_GROUPS
TOP_K = 2
D_EXPERT = D_MODEL
MOE_BLOCK = 128
EPS = 1e-6

kernel_name = 'hybrid_conv_pool_mlstm_moe_prefix_block'

def rmsnorm(x, g):
    x32 = x.astype(jnp.float32)
    y = x32 * lax.rsqrt(jnp.mean(x32 * x32, -1, keepdims=True) + EPS) * g.astype(jnp.float32)
    return y.astype(x.dtype)

def layernorm(x, g, b):
    x32 = x.astype(jnp.float32)
    mu = jnp.mean(x32, -1, keepdims=True)
    var = jnp.mean(jnp.square(x32 - mu), -1, keepdims=True)
    y = (x32 - mu) * lax.rsqrt(var + EPS) * g.astype(jnp.float32) + b.astype(jnp.float32)
    return y.astype(x.dtype)

def modulate(x, shift, scale):
    return x * (1 + scale) + shift

def dwconv(x, w, b, pad):
    y = lax.conv_general_dilated(x, w[:, None, :].astype(x.dtype), window_strides=(1,), padding=[pad],
                                 dimension_numbers=('NWC', 'WIO', 'NWC'), feature_group_count=x.shape[-1])
    return y + b

def centred_mean(x, window):
    L = x.shape[1]
    left = window // 2
    right = window - 1 - left
    cs = jnp.cumsum(x.astype(jnp.float32), axis=1)
    cs = jnp.concatenate([jnp.zeros_like(cs[:, :1]), cs], axis=1)
    pos = jnp.arange(L)
    lo = jnp.clip(pos - left, 0, L)
    hi = jnp.clip(pos + right + 1, 0, L)
    total = jnp.take(cs, hi, axis=1) - jnp.take(cs, lo, axis=1)
    cnt = (hi - lo).astype(jnp.float32).reshape((1, L) + (1,) * (x.ndim - 2))
    return (total / cnt).astype(x.dtype)

def mixer_ab(h, grid, w_in, w_dw, b_dw, ln_g, ln_b, w_pool, b_pool, pool_scale, w_out):
    B, L, _ = h.shape
    u = h @ w_in
    a = u[..., :CONV_W] * jax.nn.sigmoid(u[..., CONV_W:2 * CONV_W])
    bp = u[..., 2 * CONV_W:]
    pad = (CONV_K // 2, CONV_K // 2)
    if grid:
        rows = L // GRID_W
        a = dwconv(a.reshape(B * rows, GRID_W, CONV_W), w_dw, b_dw, pad).reshape(B, L, CONV_W)
        bp = bp.reshape(B, rows, GRID_W, POOL_GROUPS, POOL_GC)
    else:
        a = dwconv(a, w_dw, b_dw, pad)
        bp = bp.reshape(B, L, POOL_GROUPS, POOL_GC)
    a = jax.nn.silu(layernorm(a, ln_g, ln_b))
    pooled = jnp.stack([centred_mean(bp[..., g, :], w) - bp[..., g, :] for g, w in enumerate(POOL_WINDOWS)], axis=-2)
    p = jnp.einsum('...gc,gcd->...gd', pooled, w_pool) + b_pool
    p = p.reshape(B, L, POOL_W) * pool_scale
    return jnp.concatenate([a, p], axis=-1) @ w_out

def blockdiag(x, w):
    B, L, E = x.shape
    return jnp.einsum('blni,nio->blno', x.reshape(B, L, E // QKV_BLOCK, QKV_BLOCK), w).reshape(B, L, E)

def mlstm_inputs(h, w_in, w_conv, b_conv, w_q, w_k, w_v, w_gates, b_gates):
    B, L, _ = h.shape
    u = h @ w_in
    xm, z = u[..., :MLSTM_E], u[..., MLSTM_E:]
    xc = jax.nn.silu(dwconv(xm, w_conv, b_conv, (SHORT_K // 2, SHORT_K - 1 - SHORT_K // 2)))
    q = blockdiag(xc, w_q)
    k = blockdiag(xc, w_k)
    v = blockdiag(xm, w_v)
    g = (jnp.concatenate([q, k, v], axis=-1) @ w_gates + b_gates).astype(jnp.float32).reshape(B, L, 4, MLSTM_H)
    heads = lambda t: t.reshape(B, L, MLSTM_H, MLSTM_DH)
    return heads(q), heads(k) * (MLSTM_DH ** -0.5), heads(v), g, jax.nn.sigmoid(z)

def mlstm_scan(q, k, v, i_pre, f_pre, state):
    B, L, H, DH = q.shape
    nc = L // CHUNK
    chunks = lambda t: t.astype(jnp.float32).reshape(B, nc, CHUNK, H, -1).transpose(1, 0, 3, 2, 4)
    gchunks = lambda t: t.astype(jnp.float32).reshape(B, nc, CHUNK, H).transpose(1, 0, 3, 2)
    tri = jnp.tril(jnp.ones((CHUNK, CHUNK), dtype=bool))

    def step(carry, inp):
        C, n, m = carry
        qc, kc, vc, ic, lf = inp
        b = jnp.cumsum(lf, axis=-1)
        dmat = jnp.where(tri, b[..., :, None] - b[..., None, :] + ic[..., None, :], -jnp.inf)
        inter = b + m[..., None]
        m_t = jnp.maximum(inter, dmat.max(-1))
        wmat = jnp.exp(dmat - m_t[..., None])
        w_inter = jnp.exp(inter - m_t)
        s = jnp.einsum('bhtd,bhsd->bhts', qc, kc) * wmat
        num = jnp.einsum('bhts,bhse->bhte', s, vc) + w_inter[..., None] * jnp.einsum('bhtd,bhde->bhte', qc, C)
        den = s.sum(-1) + w_inter * jnp.einsum('bhtd,bhd->bht', qc, n)
        h = num / jnp.maximum(jnp.abs(den), jnp.exp(-m_t))[..., None]
        b_end = b[..., -1]
        dlog = b_end[..., None] - b + ic
        m_new = jnp.maximum(b_end + m, dlog.max(-1))
        wk = jnp.exp(dlog - m_new[..., None])
        decay = jnp.exp(b_end + m - m_new)
        C = decay[..., None, None] * C + jnp.einsum('bhsd,bhse->bhde', kc * wk[..., None], vc)
        n = decay[..., None] * n + jnp.einsum('bhs,bhsd->bhd', wk, kc)
        return (C, n, m_new), h

    state, hs = lax.scan(step, state, (chunks(q), chunks(k), chunks(v), gchunks(i_pre),
                                       gchunks(jax.nn.log_sigmoid(f_pre))))
    return hs.transpose(1, 0, 3, 2, 4).reshape(B, L, H, DH), state

def mlstm_out(hsum, o, hn_g, w_out):
    B, L, H, DH = hsum.shape
    mu = jnp.mean(hsum, -1, keepdims=True)
    var = jnp.mean(jnp.square(hsum - mu), -1, keepdims=True)
    hn = ((hsum - mu) * lax.rsqrt(var + EPS)).reshape(B, L, H * DH) * hn_g.astype(jnp.float32)
    return (o * hn.astype(o.dtype)) @ w_out

def mixer_c(h_lat, h_ctx, need_ctx, w_in, w_conv, b_conv, w_q, w_k, w_v, w_gates, b_gates, hn_g, w_out):
    prm = (w_in, w_conv, b_conv, w_q, w_k, w_v, w_gates, b_gates)
    ql, kl, vl, gl, ol = mlstm_inputs(h_lat, *prm)
    qc, kc, vc, gc, oc = mlstm_inputs(h_ctx, *prm)
    B = h_lat.shape[0]
    s0 = (jnp.zeros((B, MLSTM_H, MLSTM_DH, MLSTM_DH), jnp.float32),
          jnp.zeros((B, MLSTM_H, MLSTM_DH), jnp.float32),
          jnp.zeros((B, MLSTM_H), jnp.float32))
    flip = lambda t: jnp.flip(t, axis=1)
    hcf, sf = mlstm_scan(qc, kc, vc, gc[:, :, 0], gc[:, :, 1], s0)
    hcb, sb = mlstm_scan(flip(qc), flip(kc), flip(vc), flip(gc[:, :, 2]), flip(gc[:, :, 3]), s0)
    hlf, _ = mlstm_scan(ql, kl, vl, gl[:, :, 0], gl[:, :, 1], sf)
    hlb, _ = mlstm_scan(flip(ql), flip(kl), flip(vl), flip(gl[:, :, 2]), flip(gl[:, :, 3]), sb)
    y_lat = mlstm_out(hlf + flip(hlb), ol, hn_g, w_out)
    y_ctx = mlstm_out(hcf + flip(hcb), oc, hn_g, w_out) if need_ctx else None
    return y_lat, y_ctx

def moe(h, w_router, b_router, w1, w3, w2):
    N, D = h.shape
    scores = jax.nn.sigmoid(h.astype(jnp.float32) @ w_router.astype(jnp.float32))
    biased = (scores + b_router.astype(jnp.float32)).reshape(N, N_GROUPS, EXPERTS_PER_GROUP)
    gscore = lax.top_k(biased, 2)[0].sum(-1)
    gsel = lax.top_k(gscore, 1)[1]
    cand = jnp.take_along_axis(biased, gsel[:, :, None], axis=1)[:, 0]
    loc = lax.top_k(cand, TOP_K)[1]
    eidx = gsel * EXPERTS_PER_GROUP + loc
    wts = jnp.take_along_axis(scores, eidx, axis=1)
    wts = wts / wts.sum(-1, keepdims=True)
    A = N * TOP_K
    flat_e = eidx.reshape(A)
    order = jnp.argsort(flat_e)
    e_s = flat_e[order]
    tok_s = jnp.repeat(jnp.arange(N), TOP_K)[order]
    w_s = wts.reshape(A)[order]
    counts = jnp.bincount(flat_e, length=N_EXPERTS)
    padded = (counts + MOE_BLOCK - 1) // MOE_BLOCK * MOE_BLOCK
    pad_end = jnp.cumsum(padded)
    pad_start = pad_end - padded
    start = jnp.cumsum(counts) - counts
    dest = pad_start[e_s] + jnp.arange(A) - start[e_s]
    P = ((A + MOE_BLOCK - 1) // MOE_BLOCK + N_EXPERTS) * MOE_BLOCK
    nb = P // MOE_BLOCK
    buf = jnp.zeros((P, D), h.dtype).at[dest].set(h[tok_s])
    block_e = jnp.minimum(jnp.searchsorted(pad_end, jnp.arange(nb) * MOE_BLOCK, side='right'), N_EXPERTS - 1)

    def expert_block(args):
        xb, e = args
        return (jax.nn.silu(xb @ w1[e]) * (xb @ w3[e])) @ w2[e]

    out = lax.map(expert_block, (buf.reshape(nb, MOE_BLOCK, D), block_e)).reshape(P, D)
    return jnp.zeros((N, D), h.dtype).at[tok_s].add(out[dest] * w_s[:, None].astype(h.dtype))

def setup_inputs(seed: int = 0) -> dict:
    key = jax.random.key(seed)
    ks = list(jax.random.split(key, 40))

    def nrm(i, shape, scale):
        return jax.random.normal(ks[i], shape, jnp.float32) * scale

    D = D_MODEL
    NE, NO, E, H = N_EVEN, N_ODD, MLSTM_E, MLSTM_H
    i_bias = nrm(23, (NO, 2, 1, H), 0.1)
    f_bias = jnp.linspace(3.0, 6.0, H, dtype=jnp.float32) + nrm(24, (NO, 2, 1, H), 0.1)
    b_gates = jnp.concatenate([i_bias, f_bias], axis=2).reshape(NO, 4 * H)
    qkv_shape = (NO, E // QKV_BLOCK, QKV_BLOCK, QKV_BLOCK)
    return {
        'x': nrm(0, (BATCH, SEQ, D), 1.0),
        'c': nrm(1, (BATCH, D), 1.0),
        'ctx': nrm(2, (BATCH, CTX_LEN, D), 1.0),
        'c_ctx': nrm(3, (D,), 1.0),
        'w_ada': nrm(4, (DEPTH, D, 6 * D), 0.5 * D ** -0.5),
        'b_ada': nrm(5, (DEPTH, 6 * D), 0.02),
        'g_mix': 1.0 + nrm(6, (DEPTH, D), 0.05),
        'g_ffn': 1.0 + nrm(7, (DEPTH, D), 0.05),
        'g_final': 1.0 + nrm(8, (D,), 0.05),
        'w_in_ab': nrm(9, (NE, D, AB_IN), D ** -0.5),
        'w_dw_a': nrm(10, (NE, CONV_K, CONV_W), CONV_K ** -0.5),
        'b_dw_a': nrm(11, (NE, CONV_W), 0.02),
        'ln_g_a': 1.0 + nrm(12, (NE, CONV_W), 0.05),
        'ln_b_a': nrm(13, (NE, CONV_W), 0.02),
        'w_pool': nrm(14, (NE, POOL_GROUPS, POOL_GC, POOL_GC), POOL_GC ** -0.5),
        'b_pool': nrm(15, (NE, POOL_GROUPS, POOL_GC), 0.02),
        'pool_scale': 1.0 + nrm(16, (NE, POOL_W), 0.1),
        'w_out_ab': nrm(17, (NE, AB_OUT, D), AB_OUT ** -0.5),
        'w_in_c': nrm(18, (NO, D, 2 * E), D ** -0.5),
        'w_conv_c': nrm(19, (NO, SHORT_K, E), SHORT_K ** -0.5),
        'b_conv_c': nrm(20, (NO, E), 0.02),
        'w_q': nrm(21, qkv_shape, QKV_BLOCK ** -0.5),
        'w_k': nrm(22, qkv_shape, QKV_BLOCK ** -0.5),
        'w_v': nrm(25, qkv_shape, QKV_BLOCK ** -0.5),
        'w_gates': nrm(26, (NO, 3 * E, 4 * H), (3 * E) ** -0.5),
        'b_gates': b_gates,
        'hn_g': 1.0 + nrm(27, (NO, E), 0.05),
        'w_out_c': nrm(28, (NO, E, D), E ** -0.5),
        'w_router': nrm(29, (D, N_EXPERTS), D ** -0.5),
        'b_router': nrm(30, (N_EXPERTS,), 0.01),
        'w1': nrm(31, (DEPTH, N_EXPERTS, D, D_EXPERT), D ** -0.5),
        'w3': nrm(32, (DEPTH, N_EXPERTS, D, D_EXPERT), D ** -0.5),
        'w2': nrm(33, (DEPTH, N_EXPERTS, D_EXPERT, D), D_EXPERT ** -0.5),
    }

def reference(x, c, ctx, c_ctx, w_ada, b_ada, g_mix, g_ffn, g_final, w_in_ab, w_dw_a, b_dw_a, ln_g_a, ln_b_a,
              w_pool, b_pool, pool_scale, w_out_ab, w_in_c, w_conv_c, b_conv_c, w_q, w_k, w_v, w_gates, b_gates,
              hn_g, w_out_c, w_router, b_router, w1, w3, w2):
    B, S, D = x.shape
    n_ctx = B * ctx.shape[1]
    x_lat, x_ctx = x, ctx
    sc = jax.nn.silu(c)
    scc = jax.nn.silu(c_ctx)
    for l in range(DEPTH):
        last = l == DEPTH - 1
        even = l % 2 == 0
        j = l // 2
        mod_lat = jnp.split((sc @ w_ada[l] + b_ada[l])[:, None, :], 6, axis=-1)
        mod_ctx = jnp.split((scc @ w_ada[l] + b_ada[l])[None, None, :], 6, axis=-1)
        h_lat = modulate(rmsnorm(x_lat, g_mix[l]), mod_lat[0], mod_lat[1])
        if even:
            prm = (w_in_ab[j], w_dw_a[j], b_dw_a[j], ln_g_a[j], ln_b_a[j], w_pool[j], b_pool[j], pool_scale[j], w_out_ab[j])
            y_lat = mixer_ab(h_lat, True, *prm)
            if not last:
                h_ctx = modulate(rmsnorm(x_ctx, g_mix[l]), mod_ctx[0], mod_ctx[1])
                y_ctx = mixer_ab(h_ctx, False, *prm)
        else:
            h_ctx = modulate(rmsnorm(x_ctx, g_mix[l]), mod_ctx[0], mod_ctx[1])
            y_lat, y_ctx = mixer_c(h_lat, h_ctx, not last, w_in_c[j], w_conv_c[j], b_conv_c[j], w_q[j], w_k[j],
                                   w_v[j], w_gates[j], b_gates[j], hn_g[j], w_out_c[j])
        x_lat = x_lat + mod_lat[2] * y_lat
        h_lat = modulate(rmsnorm(x_lat, g_ffn[l]), mod_lat[3], mod_lat[4])
        if last:
            y = moe(h_lat.reshape(B * S, D), w_router, b_router, w1[l], w3[l], w2[l])
            x_lat = x_lat + mod_lat[5] * y.reshape(B, S, D)
        else:
            x_ctx = x_ctx + mod_ctx[2] * y_ctx
            h_ctx = modulate(rmsnorm(x_ctx, g_ffn[l]), mod_ctx[3], mod_ctx[4])
            y = moe(jnp.concatenate([h_ctx.reshape(n_ctx, D), h_lat.reshape(B * S, D)], axis=0),
                    w_router, b_router, w1[l], w3[l], w2[l])
            x_ctx = x_ctx + mod_ctx[5] * y[:n_ctx].reshape(x_ctx.shape)
            x_lat = x_lat + mod_lat[5] * y[n_ctx:].reshape(B, S, D)
    return rmsnorm(x_lat, g_final)


_drawn_inputs = setup_inputs


def setup_inputs(seed=0):
    import zlib

    import numpy as np

    out = dict(_drawn_inputs(seed))
    spreads = {}
    factors = {'ln_b_a': 3.525, 'b_conv_c': 3.539, 'hn_g': 2.933, 'b_dw_a': 2.969, 'b_pool': 2.838}
    for name, (base, spread) in spreads.items():
        noise = np.random.default_rng([zlib.crc32(name.encode()), seed]).standard_normal(out[name].shape)
        drawn = base * np.exp(spread * noise) if base else spread * noise
        out[name] = jnp.asarray(drawn.astype(out[name].dtype))
    for name, factor in factors.items():
        out[name] = (out[name] * factor).astype(out[name].dtype)
    return out
```

```python
from contextlib import ExitStack

import numpy as np
import concourse.bass as bass
from concourse import mybir

F32 = mybir.dt.float32
F32R = mybir.dt.float32r
I32 = mybir.dt.int32
ALU = mybir.AluOpType
ACT = mybir.ActivationFunctionType
AX = mybir.AxisListType

P = 128
D = 1024
KD = D // P
S_CTX, S_LAT = 256, 512
S = S_CTX + S_LAT
NT = S // P
CT = S_CTX // P
E2 = 2 * D
KE = E2 // P
H, DH = 4, 512
HC = DH // P
GRID_W = 64
ROWS = S // GRID_W
CROWS = S_CTX // GRID_W
LROWS = ROWS - CROWS
RC = S_CTX + LROWS
TAPS, HALO = 31, 15
RW = GRID_W + 2 * HALO
PH = 8
PW = GRID_W + 2 * PH
WINDOWS = (2, 4, 8, 16)
NPAR = TAPS + 5
NX = 16
A_MAX = 2 * S
EXTRA = (A_MAX - 1) // P
NB = NX + EXTRA + 1
FMAX = S // P - 1
EPS = 1e-6
NEG = -1e30
BIG = 65536.0
XC = S + 2
XM = S + 5

CHAINS = []
for _n, _tiles in enumerate((range(NT), range(NT), range(NT), range(CT, NT), range(CT, NT))):
    for _t in _tiles:
        CHAINS.append((_n, _t, len(CHAINS)))


def tiles_of(n):
    return [(t, j) for m, t, j in CHAINS if m == n]


C_ID, C_TRI, C_NF, C_NB_, C_G4 = 0, 128, 256, 384, 512
C_TIE, C_E, C_J, C_TH = 544, 560, 576, 592
C_END = 600


def constants():
    c = np.zeros((P, C_END), np.float32)
    i = np.arange(P)
    c[:, C_ID:C_ID + P] = np.eye(P)
    c[:, C_TRI:C_TRI + P] = i[:, None] < i[None, :]
    c[:, C_NF:C_NF + P] = np.where(i[None, :] <= i[:, None], 0.0, NEG)
    c[:, C_NB_:C_NB_ + P] = np.where(i[None, :] >= i[:, None], 0.0, NEG)
    c[:, C_G4:C_G4 + 32] = np.arange(32)[None, :] == (i // 4)[:, None]
    c[:, C_TIE:C_TIE + 16] = (np.arange(4)[None, :] < np.arange(4)[:, None]).reshape(1, 16)
    c[:, C_E:C_E + NX] = np.arange(NX)
    c[:, C_J:C_J + 16] = np.arange(16)
    c[:, C_TH:C_TH + FMAX] = P * (1 + np.arange(FMAX))
    rc = np.zeros((4, RC), np.float32)
    for w_i, w in enumerate(WINDOWS):
        left, right = w // 2, w - 1 - w // 2
        for base, total, length in ((0, S_CTX, S_CTX), (S_CTX, LROWS, LROWS)):
            pos = np.arange(total)
            rc[w_i, base:base + total] = 1.0 / (np.minimum(pos + right + 1, length) - np.maximum(pos - left, 0))
    return c, rc.reshape(1, -1)


def bc(ap, axis, n):
    a = ap.unsqueeze(axis)
    shape = list(a.shape)
    shape[axis] = n
    return a.broadcast_to(shape)



def program(nc, x, c, ctx_in, c_ctx, w_ada, b_ada, g_mix, g_ffn, g_final, w_in_ab, w_dw_a, b_dw_a, ln_g_a, ln_b_a,
            w_pool, b_pool, pool_scale, w_out_ab, w_in_c, w_conv_c, b_conv_c, w_q, w_k, w_v, w_gates, b_gates,
            hn_g, w_out_c, w_router, b_router, w1, w3, w2, consts, rcounts, out):
    def dram(name, shape):
        return nc.dram_tensor(name, shape, F32, kind="Internal").ap()

    mods_d = dram("mods_d", [2, 2, 6 * D])
    xs_d = [None] + [dram(f"xs{n}_d", [S, D]) for n in (1, 2, 3)]
    buf_d = dram("buf_d", [P * NB, D])
    zs_d = dram("zs_d", [S_LAT, E2])
    arow_d = dram("arow_d", [2 * H, S])
    buf_v = buf_d.rearrange("(p b) d -> p b d", b=NB)

    es = ExitStack()
    with es:
        def sb(name, shape, dt=F32):
            return es.enter_context(nc.sbuf_tensor(name, shape, dt))

        def sem(name):
            return es.enter_context(nc.semaphore(name))

        def sems(names):
            return [sem(s) for s in names.split()]

        base = 0
        while base < nc.sbuf_base:
            base += 64
        arena = nc.alloc_sbuf_tensor_at("arena", [P, AR], F32, offset=base)
        fence = sb("fence", [P, AR + 16])
        cst = sb("cst", [P, C_END])
        ones = sb("ones", [P, P])
        onesd = sb("onesd", [P, P])
        par = sb("par", [P, KD, NPAR])
        pscb = sb("pscb", [P, KD])
        par2 = sb("par2", [P, KE, 5])
        gbias = sb("gbias", [P, 1])
        epsc = sb("epsc", [P, 1])
        ss = sb("ss", [P, 2])
        rt = sb("rt", [P, 2])
        rs = sb("rs", [P, 2])
        wrt = sb("wrt", [P, KD, NX])
        brow = sb("brow", [P, NX])
        slots = sb("slots", [P, 2, NT], I32)
        wsel = sb("wsel", [P, 2, NT])
        table = sb("table", [1, 32], I32)
        st = sb("st", [P, 2, 4, 2, H])
        dn = sb("dn", [P, 2, 16])
        bst = sb("bst", [P, 2, 16])
        ps = es.enter_context(nc.psum_tensor("ps", [P, 8, 512], F32))
        psf = ps[:].rearrange("p b n -> p (b n)")

        def at(off, *dims):
            n = int(np.prod(dims))
            a = arena[:, off:off + n]
            assert off + n <= AR, (off, dims)
            if len(dims) == 2:
                a = a.rearrange("p (a b) -> p a b", a=dims[0])
            if len(dims) == 3:
                a = a.rearrange("p (a b c) -> p a b c", a=dims[0], b=dims[1])
            return a

        def rounded(name, off, *dims):
            return nc.alloc_sbuf_tensor_at(name, [P, *dims], F32R, offset=base + 4 * off)[:]

        ident = cst[:, C_ID:C_ID + P]

        s_cst, s_c, s_bada, s_one, s_ct, s_sc = sems("s_cst s_c s_bada s_one s_ct s_sc")
        ada_w = [sem(f"ada_w{i}") for i in range(NW)]
        ada_mm, ada_row, ada_all = sems("ada_mm ada_row ada_all")
        ada_st = [sem(f"ada_st{i}") for i in range(NW)]
        par_in, par_tr, par_rdy = sems("par_in par_tr par_rdy")
        s_mod = sem("s_mod")
        xt_in, xt_st, y_in, out_st = ([sem(f"{s}{i}") for i in range(2)] for s in ("xt_in", "xt_st", "y_in", "out_st"))
        y_mm, x_new, ss_rdy, rt_rdy, h_rdy, tr_rdy, ht_rdy, lg_rdy = sems(
            "y_mm x_new ss_rdy rt_rdy h_rdy tr_rdy ht_rdy lg_rdy")
        dv = sem("dv")
        wr_in, sc_rdy, mk_rdy, pos_rdy, sl_rdy, s_fill, s_scat = sems("wr_in sc_rdy mk_rdy pos_rdy sl_rdy s_fill s_scat")
        abw = sems("abw0 abw1")
        wo_in = sems("wo_in0 wo_in1 wo_in2 wo_in3")
        rc_in, wp_in, ab_u, sg_rdy, glu_done, conv_s = sems("rc_in wp_in ab_u sg_rdy glu_done conv_s")
        pl_u, bp_rdy, pool_s, pg_mm, p_rdy, pad_z = sems("pl_u bp_rdy pool_s pg_mm p_rdy pad_z")
        ln_mu, ln_d, ln_sq, ln_sm, ln_ve, ln_sd, ln_n, ln_y = sems("ln_mu ln_d ln_sq ln_sm ln_ve ln_sd ln_n ln_y")
        moe = []
        for l in range(2):
            m = {s: sem(f"m{l}_{s}") for s in "used high low xg tx ab si g tg ye yst done".split()}
            m["w"] = [sem(f"m{l}_w{i}") for i in range(6)]
            moe.append(m)
        cw = sems("cw0 cw1")
        xm_z, xm_mm, cv_s, xc_rdy, z_mm, z_rdy = sems("xm_z xm_mm cv_s xc_rdy z_mm z_rdy")
        z_st = sems("z_st0 z_st1")
        raw_in, bd_rdy, bt_mm, bt_ev, ge_mm, ge_rdy, g_mm, gr, ga, ar_st, stt_mm, st_rdy = sems(
            "raw_in bd_rdy bt_mm bt_ev ge_mm ge_rdy g_mm gr ga ar_st stt_mm st_rdy")
        v_mm, v_ev, kq_mm, k_ev, q_ev = sems("v_mm v_ev kq_mm k_ev q_ev")
        ab_in, hn_in = sems("ab_in hn_in")
        zl_in = sems("zl_in0 zl_in1")
        sS, dg, eE, aA, tT, aT, pV, lV, lX, hV, yT_mm, yT_ev = sems("sS dg eE aA tT aT pV lV lX hV yT_mm yT_ev")

        hT = at(0, KD, S)
        hall = at(0, NT, D)
        catT = at(6144, 2 * KD, S)
        ring = [at(18432 + 4096 * i, KD, 512) for i in range(2)]
        wo = [at(26624, 2 * KD, 512), at(18432, 2 * KD, 512)]
        apad = [at(34816 + ROWS * RW * i, ROWS, RW) for i in range(2)]
        lpad = [at(37072 + 1536 * i, LROWS + 2 * PH, GRID_W) for i in range(2)]
        bpad = [at(40144 + 320 * i, CROWS, PW) for i in range(2)]
        ltmp = [at(o, LROWS + 2 * PH, GRID_W) for o in (40912, 6144 + 14 * S)]
        btmp = [at(o, CROWS, PW) for o in (40912, 6144 + 14 * S)]
        acc1 = at(42448, S)
        lnv = at(0, S)
        pooled = [at(43216 + S * i, S) for i in range(4)]
        rcnt = at(46288, 4, RC)
        wpool = at(47568, 8, 256)
        sg = [at(49616 + S * i, S) for i in range(2)]

        def chain_arrays(n):
            if n == 3:
                return dict(xt=[at(22528 + D * i, D) for i in range(2)],
                            mod=[None] * 3 + [at(24576 + D * i, D) for i in range(3)],
                            tmp=at(27648, D), htt=at(28672, KD, P))
            return dict(xt=[at(34928 + D * i, D) for i in range(2)],
                        mod=[at(36976 + D * i, D) for i in range(6)],
                        tmp=at(43120, D), htt=at(44144, KD, P),
                        h=[at(6144 + D * i, D) for i in range(2)],
                        y=[[at(8192 + D * (2 * k + i), D) for i in range(2)] for k in range(2)])

        CH = [chain_arrays(n) for n in range(5)]
        MOD_OF = {0: ((0, 0), None), 1: ((0, 3), (0, 2)), 2: ((1, 0), (0, 5)), 3: ((1, 3), (1, 2)), 4: (None, (1, 5))}
        G_OF = {0: g_mix[0], 1: g_ffn[0], 2: g_mix[1], 3: g_ffn[1], 4: g_final}
        MODS = []
        for n in range(5):
            per = (2 if MOD_OF[n][0] else 0) + (1 if MOD_OF[n][1] else 0)
            MODS.append((MODS[-1] if MODS else 0) + 16 * (1 + per * (1 if n >= 3 else 2)))

        R0 = 45184
        r_sc, r_bi, r_m, r_t, r_w, r_f, r_sl, r_pos = (at(R0 + 96 * i, NT, NX) for i in range(8))
        r_big, r_big2 = at(R0 + 768, 480), at(R0 + 1248, 480)
        r_s = at(R0 + 1728, 400)

        wx = nc.alloc_sbuf_tensor_at("wx", [P, 6, 2, D], F32, offset=base + 4 * 6144)[:]
        wh = rounded("wh", 18432, NHL, D)
        wl = rounded("wl", 18432 + NHL * D, NHL, D)
        xg, gg, s0, yy = (at(D * i, D) for i in range(4))
        xTh, xTl = (rounded(f"xT{i}", 4 * D + D * i, KD, P) for i in range(2))
        gTh, gTl = (rounded(f"gT{i}", 45184 + D * i, KD, P) for i in range(2))

        adaw = [at(4096 * i, KD, 512) for i in range(NW)]
        bada = at(16384, 12 * D)
        stage = [at(28672 + 512 * i, 512) for i in range(NW)]
        csrc = at(30720, P)
        scT = at(30848, 2 * KD)
        psrc = at(30976, D)
        psrc2 = at(32000, E2)
        zt = at(44144, D)

        A_XM, A_XC = 6144, 6144 + KE * XM
        xm = at(A_XM, KE, XM)
        xc = at(A_XC, KE, XC)
        cring = [at(30832 + 4096 * i, KD, 512) for i in range(2)]
        BD = at(39024, 3, KE, P)
        geff = at(45168, 2 * KE, P)
        zst = [at(49264 + 512 * i, 512) for i in range(2)]
        raw = at(50288, 3, KE, 4)
        bdt = [at(30832 + 512 * i, 4, P) for i in range(2)]
        wg = at(31856, 3 * KE, NX)
        G, r_lf, r_b, r_a, r_M, r_x, r_zero = (at(32768 + S * i, S) for i in range(7))
        r_fl = at(30832, S)
        abc = at(0, 2 * H, S)
        qT = at(30832, KE, S_LAT)
        vv = [at(A_XM + HC * XM * h, NT, DH) for h in range(H)]
        Ef, Eb, A0, A1, AT = (at(45168 + S * i, S) for i in range(5))
        AA = [A0, A1]
        hv = at(49008, DH)
        zl = [at(49520 + DH * i, DH) for i in range(2)]
        hn = at(50544, DH)
        woc = [at(6144, KE, 512), at(14336, KE, 512)]

        w_ada_v = [w_ada[l].rearrange("(k p) n -> p k n", p=P) for l in range(2)]
        NA = 6 * D // 512

        def ada_groups(eng):
            yield 0, 0, None
            with eng.Fori(1, NA // NW) as g:
                yield 0, g * NW, g * NW
            with eng.Fori(0, NA // NW) as g:
                yield 1, g * NW, g * NW + NA

        block = es.enter_context(nc.Block())

        def stores(n_to, j_to, s):
            return sum(1 for m, t, j in CHAINS if m in (1, 2, 3) and j % 2 == s and (m < n_to or j <= j_to))

        @block.sync
        def _(sp):
            sp.dma_start(cst[:], consts).then_inc(s_cst, 16)
            sp.dma_start(csrc[0:KD, :], c.rearrange("a (k p) -> (a k) p", p=P)).then_inc(s_c, 16)
            sp.dma_start(csrc[KD:2 * KD, :], c_ctx.rearrange("(k p) -> k p", p=P)).then_inc(s_c, 16)
            sp.dma_start(wrt[:], w_router.rearrange("(k p) n -> p k n", p=P)).then_inc(wr_in, 16)
            sp.dma_start(brow[:], b_router.partition_broadcast(P)).then_inc(wr_in, 16)
            for v in range(2):
                sp.dma_start(bada[v:v + 1, :], b_ada.rearrange("l n -> (l n)").unsqueeze(0)).then_inc(s_bada, 16)
            for l, n, i in ada_groups(sp):
                for s in range(NW):
                    if i is not None:
                        sp.wait_ge(ada_mm, i + s - NW + 1)
                    src = w_ada_v[l][:, :, n * 512 + s * 512:n * 512 + s * 512 + 512] if i is None else \
                        w_ada_v[l][:, :, bass.ds(n * 512 + s * 512, 512)]
                    sp.dma_start(adaw[s], src).then_inc(ada_w[s], 16)
                if i is None:
                    sp.dma_start(psrc[0:TAPS, :], w_dw_a[0]).then_inc(par_in, 16)
                    for r, v in enumerate((b_dw_a, ln_g_a, ln_b_a, b_pool.rearrange("a g d -> a (g d)"), pool_scale)):
                        sp.dma_start(psrc[TAPS + r:TAPS + r + 1, :], v).then_inc(par_in, 16)
                    sp.dma_start(psrc2[0:4, :], w_conv_c[0]).then_inc(par_in, 16)
                    sp.dma_start(psrc2[4:5, :], b_conv_c).then_inc(par_in, 16)

            def load_mods(n):
                m = CH[n]["mod"]
                ss_, gate = MOD_OF[n]
                for v in range(1 if n >= 3 else 2):
                    o = 3 * (1 - v)
                    if ss_:
                        l, r = ss_
                        sp.dma_start(m[o], mods_d[l, v, (r + 1) * D:(r + 2) * D].partition_broadcast(P)).then_inc(s_mod, 16)
                        sp.dma_start(m[o + 1], mods_d[l, v, r * D:(r + 1) * D].partition_broadcast(P)).then_inc(s_mod, 16)
                    if gate:
                        l, r = gate
                        sp.dma_start(m[o + 2], mods_d[l, v, r * D:(r + 1) * D].partition_broadcast(P)).then_inc(s_mod, 16)
                sp.dma_start(CH[n]["tmp"], G_OF[n].partition_broadcast(P)).then_inc(s_mod, 16)

            def load_x(n, t, j):
                if n < 2:
                    src = ctx_in[0, t * P:(t + 1) * P, :] if t < CT else x[0, (t - CT) * P:(t - CT + 1) * P, :]
                else:
                    src = xs_d[n - 1][t * P:(t + 1) * P, :]
                sp.dma_start(CH[n]["xt"][j % 2], src).then_inc(xt_in[j % 2], 16)

            def chain_start(n):
                for s in range(2):
                    if stores(n, -1, s):
                        sp.wait_ge(xt_st[s], 16 * stores(n, -1, s))
                load_mods(n)
                for t, j in tiles_of(n)[:2]:
                    load_x(n, t, j)

            def chain(n):
                tiles = tiles_of(n)
                for i, (t, j) in enumerate(tiles):
                    s = j % 2
                    if n in (1, 2, 3):
                        sp.wait_ge(x_new, j + 1 - NT)
                        sp.dma_start(xs_d[n][t * P:(t + 1) * P, :], CH[n]["xt"][s]).then_inc(xt_st[s], 16)
                    if n == 4:
                        sp.wait_ge(h_rdy, j + 1)
                        sp.dma_start(out[0, (t - CT) * P:(t - CT + 1) * P, :], CH[4]["h"][s]).then_inc(out_st[s], 16)
                    if i + 2 < len(tiles):
                        sp.wait_ge(h_rdy, j + 1)
                        if n in (1, 2, 3):
                            sp.wait_ge(xt_st[s], 16 * stores(0, j, s))
                        load_x(n, *tiles[i + 2])

            def expert_weights(l, e, b, groups, ahead=0):
                m = moe[l]
                for g in groups:
                    kk, mat = (g // 2, (w1, w3)[g % 2]) if g < 8 else (g - 8, w2)
                    if g >= 6:
                        sp.wait_ge(m["low"], made(b, "chunk", 2 * g - 11))
                    elif b is not None:
                        sp.wait_ge(m["low"], made(b, "chunk", 2 * g + 13, PARTS * (ahead - 1)))
                    src = mat[l].rearrange("e (k p) n -> p (e k) n", p=P)[:, bass.ds(e * KD + 2 * kk, 2), :]
                    sp.dma_start(wx[:, g % 6], src).then_inc(m["w"][g % 6], 16)

            def experts(l):
                expert_weights(l, 0, None, range(6, 12))
                sp.wait_ge(sl_rdy, l + 1)
                nb = sp.value_load(table[0:1, 31:32], min_val=NX, max_val=NB - 1)
                expert_weights(l, 1, 0, range(2), 1)
                with sp.Fori(1, nb) as b:
                    e = sp.value_load(table[0:1, bass.ds(b, 1)], min_val=0, max_val=NX - 1)
                    after = sp.value_load(table[0:1, bass.ds(b + 1, 1)], min_val=0, max_val=NX - 1)
                    expert_weights(l, e, b, range(2, 12))
                    expert_weights(l, after, b, range(2), 1)

            sp.wait_ge(ada_all, 1)
            chain_start(0)
            wi = w_in_ab[0].rearrange("(k p) n -> p k n", p=P)
            woa = w_out_ab[0].rearrange("(k p) n -> p k n", p=P)

            def panel(g):
                if g < 4:
                    for q in range(2):
                        sp.dma_start(ring[g % 2][:, :, 256 * q:256 * q + 256],
                                     wi[:, :, q * D + g * 256:q * D + (g + 1) * 256]).then_inc(abw[g % 2], 16)
                else:
                    sp.dma_start(ring[g % 2], wi[:, :, 2 * D + (g - 4) * 512:2 * D + (g - 3) * 512]).then_inc(abw[g % 2], 16)

            panel(0)
            panel(1)
            chain(0)
            sp.dma_start(rcnt, rcounts.rearrange("a (w s) -> (a w) s", w=4).partition_broadcast(P)).then_inc(rc_in, 16)
            sp.dma_start(wpool, w_pool[0].rearrange("g (k p) n -> p (g k) n", p=P)).then_inc(wp_in, 16)
            for q in range(2):
                sp.dma_start(wo[0][:, 8 * q:8 * q + 8, :], woa[:, 8 * q:8 * q + 8, 0:512]).then_inc(wo_in[q], 16)
            for g in range(2, 6):
                sp.wait_ge(ab_u, 2 * (g - 1))
                panel(g)
            sp.wait_ge(pl_u, 8)
            for q in range(2):
                sp.dma_start(wo[1][:, 8 * q:8 * q + 8, :], woa[:, 8 * q:8 * q + 8, 512:1024]).then_inc(wo_in[2 + q], 16)
            sp.wait_ge(conv_s, CONV_OPS * KD)
            sp.wait_ge(p_rdy, KD)
            chain_start(1)
            chain(1)
            sp.wait_ge(y_mm, NT)
            expert_weights(0, 0, None, range(6))
            sp.wait_ge(h_rdy, 2 * NT)
            chain_start(2)
            experts(0)
            wc = w_in_c[0].rearrange("(k p) n -> p k n", p=P)
            sp.wait_ge(moe[0]["done"], 1)
            sp.dma_start(cring[0], wc[:, :, 0:512]).then_inc(cw[0], 16)
            chain(2)
            sp.wait_ge(h_rdy, 3 * NT)
            for s in range(2):
                sp.wait_ge(xt_st[s], 16 * stores(3, -1, s))
            sp.dma_start(cring[1], wc[:, :, 512:1024]).then_inc(cw[1], 16)
            for i, (wm) in enumerate((w_q, w_k, w_v)):
                sp.dma_start(raw[:, i], wm[0].rearrange("(t n) i o -> (n i) t o", n=32)).then_inc(raw_in, 16)
            for i in range(4):
                sp.dma_start(gbias[32 * i:32 * i + H, :],
                             b_gates[0, GATE_COL[i] * H:(GATE_COL[i] + 1) * H].unsqueeze(1)).then_inc(raw_in, 16)
            for g in range(2, 8):
                sp.wait_ge(xm_mm, 4 * (g - 1)) if g < 6 else sp.wait_ge(z_mm, 4 * (g - 5))
                sp.dma_start(cring[g % 2], wc[:, :, g * 512:(g + 1) * 512]).then_inc(cw[g % 2], 16)
            sp.wait_ge(z_mm, 16)
            sp.dma_start(wg, w_gates[0].rearrange("(k p) n -> p k n", p=P)).then_inc(wp_in, 16)
            sp.wait_ge(gr, R_A)
            for d in range(2):
                sp.dma_start(arow_d[4 * d:4 * d + 4, :], r_a[32 * d:32 * d + 4, :]).then_inc(ar_st, 16)
            sp.wait_ge(ar_st, 32)
            sp.dma_start(abc.rearrange("p a b -> p (a b)"),
                         arow_d.rearrange("a b -> (a b)").partition_broadcast(P)).then_inc(ab_in, 16)
            for s in range(2):
                sp.wait_ge(z_st[s], 16 * 8)
            for u in range(16):
                h, i = u // 4, u % 4
                if u == 0:
                    sp.wait_ge(g_mm, 1)
                if u >= 2:
                    sp.wait_ge(hV, u - 1)
                sp.dma_start(zl[u % 2], zs_d[i * P:(i + 1) * P, h * DH:(h + 1) * DH]).then_inc(zl_in[u % 2], 16)
                if i == 0:
                    if h:
                        sp.wait_ge(hV, u)
                    sp.dma_start(hn, hn_g[0, h * DH:(h + 1) * DH].partition_broadcast(P)).then_inc(hn_in, 16)
                if u == 13:
                    sp.wait_ge(pV, 12)
                    wov = w_out_c[0].rearrange("(k p) n -> p k n", p=P)
                    for q in range(2):
                        sp.dma_start(woc[0][:, 8 * q:8 * q + 8, :], wov[:, 8 * q:8 * q + 8, 0:512]).then_inc(wo_in[q], 16)
            sp.wait_ge(pV, 16)
            for q in range(2):
                sp.dma_start(woc[1][:, 8 * q:8 * q + 8, :], wov[:, 8 * q:8 * q + 8, 512:1024]).then_inc(wo_in[2 + q], 16)
            chain_start(3)
            chain(3)
            sp.wait_ge(y_mm, NT + 4)
            expert_weights(1, 0, None, range(6))
            chain_start(4)
            experts(1)
            chain(4)
            for s in range(2):
                sp.wait_ge(out_st[s], 32)

        @block.gpsimd
        def _(pool):
            pool.memset(zt, 0.0).then_inc(pad_z, 1)
            pool.wait_ge(pad_z, 1)
            pool.wait_ge(ada_mm, 2 * NA)
            pool.dma_start(buf_v[:, :, :], bc(zt, 1, NB)).then_inc(s_fill, 16)
            pool.wait_ge(h_rdy, NT)
            for i in range(2):
                pool.memset(apad[i], 0.0).then_inc(pad_z, 1)
                pool.memset(bpad[i], 0.0).then_inc(pad_z, 1)
                pool.memset(lpad[i], 0.0).then_inc(pad_z, 1)
            pool.wait_ge(s_fill, 16)
            pool.wait_ge(rc_in, 16)
            pool.wait_ge(pad_z, 7)
            n = 0

            def step(ins):
                nonlocal n
                n += 1
                ins.then_inc(pool_s, 1)
                pool.wait_ge(pool_s, n)

            for p in range(KD):
                g = p // 2
                b = bpad[p % 2]
                pool.wait_ge(bp_rdy, p + 1)
                if p >= 4 and p % 2 == 0:
                    pool.wait_ge(pg_mm, p - 2)
                step(pool.tensor_copy(b[:, 0:CROWS - 1, PH + GRID_W:PW], b[:, 1:CROWS, PH:2 * PH]))
                step(pool.tensor_copy(b[:, 1:CROWS, 0:PH], b[:, 0:CROWS - 1, GRID_W:GRID_W + PH]))
                win = WINDOWS[g]
                dst = pooled[p % 4].rearrange("p (r w) -> p r w", w=GRID_W)
                cur, first = lpad[p % 2], PH - win // 2
                for lv in range(g + 1):
                    nxt, w_ = ltmp[lv % 2], 1 << lv
                    rows = LROWS + win - 2 * w_
                    step(pool.tensor_tensor(nxt[:, 0:rows], cur[:, first:first + rows],
                                            cur[:, first + w_:first + w_ + rows], ALU.add))
                    cur, first = nxt, 0
                step(pool.tensor_tensor(dst[:, CROWS:], cur[:, 0:LROWS], bc(rcnt[:, g, S_CTX:], 2, GRID_W), ALU.mult))
                step(pool.tensor_tensor(dst[:, CROWS:], dst[:, CROWS:], lpad[p % 2][:, PH:PH + LROWS], ALU.subtract))
                cur, first, wdt = b, PH - win // 2, GRID_W + win
                for lv in range(g + 1):
                    nxt, w_ = btmp[lv % 2], 1 << lv
                    wdt = GRID_W + win - 2 * w_
                    step(pool.tensor_tensor(nxt[:, :, 0:wdt], cur[:, :, first:first + wdt],
                                            cur[:, :, first + w_:first + w_ + wdt], ALU.add))
                    cur, first = nxt, 0
                step(pool.tensor_tensor(dst[:, 0:CROWS], cur[:, :, 0:GRID_W],
                                        rcnt[:, g, 0:S_CTX].rearrange("p (r w) -> p r w", w=GRID_W), ALU.mult))
                step(pool.tensor_tensor(dst[:, 0:CROWS], dst[:, 0:CROWS], b[:, :, PH:PH + GRID_W], ALU.subtract))
                assert n == POOL_DONE[p]

            def scatter(l):
                pool.wait_ge(sl_rdy, l + 1)
                tl = tiles_of(1 + 2 * l)
                for k in range(2):
                    for t, j in tl:
                        pool.indirect_dma_start(buf_d, bass.IndirectOffsetOnAxis(ap=slots[:, k, t:t + 1], axis=0),
                                                hall[:, t, :], None).then_inc(s_scat, 16)

            def experts(l):
                m = moe[l]
                pool.wait_ge(s_scat, 16 * 2 * (NT if l == 0 else NT + 4))
                pool.dma_start(xg, buf_v[:, 0, :]).then_inc(m["xg"], 16)
                pool.wait_ge(m["ye"], 1)
                pool.dma_start(buf_v[:, NB - 1, 0:16], yy[:, 0:16]).then_inc(m["yst"], 16)
                nb = pool.value_load(table[0:1, 31:32], min_val=NX, max_val=NB - 1)
                with pool.Fori(0, nb) as b:
                    pool.wait_ge(m["tx"], b + 1)
                    pool.dma_start(xg, buf_v[:, bass.ds(b + 1, 1), :].rearrange("p a d -> p (a d)")).then_inc(m["xg"], 16)
                    pool.wait_ge(m["ye"], b + 2)
                    pool.dma_start(buf_v[:, bass.ds(b, 1), :].rearrange("p a d -> p (a d)"), yy).then_inc(m["yst"], 16)

            def gather(n):
                pool.wait_ge(moe[n // 2 - 1]["done"], 1)
                for t, j in tiles_of(n):
                    s = j % 2
                    if j - 2 >= tiles_of(n)[0][1]:
                        pool.wait_ge(x_new, j - 1 - NT)
                    for k in range(2):
                        pool.indirect_dma_start(CH[n]["y"][k][s], None, buf_d,
                                                bass.IndirectOffsetOnAxis(ap=slots[:, k, t:t + 1], axis=0)
                                                ).then_inc(y_in[s], 16)

            scatter(0)
            experts(0)
            gather(2)
            pool.wait_ge(tr_rdy, 3 * NT)
            pool.memset(xm[:, :, 0:2], 0.0).then_inc(xm_z, 1)
            pool.memset(xm[:, :, 2 + S_CTX:4 + S_CTX], 0.0).then_inc(xm_z, 1)
            pool.memset(xm[:, :, XM - 1:XM], 0.0).then_inc(xm_z, 1)
            pool.memset(geff, 0.0).then_inc(xm_z, 1)
            pool.wait_ge(raw_in, 48 + 64)
            for i in range(3):
                for t in range(KE):
                    ins = pool.tensor_tensor(BD[:, i, t].rearrange("p (g o) -> p g o", o=4),
                                             bc(cst[:, C_G4:C_G4 + 32], 2, 4), bc(raw[:, i, t], 1, 32), ALU.mult)
                ins.then_inc(bd_rdy, 1)
            pool.wait_ge(ab_in, 16)
            for u in range(16):
                h, i = u // 4, u % 4
                o = S_CTX + P * i
                if u == 0:
                    pool.wait_ge(g_mm, 1)
                else:
                    pool.wait_ge(aA, 4 * u)
                pool.tensor_tensor(Ef[:, o:o + P], abc[:, h, o:o + P], cst[:, C_NF:C_NF + P], ALU.add).then_inc(dg, 1)
                pool.tensor_tensor(Eb[:, o:o + P], abc[:, H + h, o:o + P], cst[:, C_NB_:C_NB_ + P], ALU.add).then_inc(dg, 1)
            scatter(1)
            experts(1)
            gather(4)

        @block.tensor
        def _(pe):
            def mm(bank_ap, lhsT, rhs, first, last):
                return pe.matmul(bank_ap, lhsT, rhs, start=first, stop=last)

            pe.wait_ge(s_cst, 16)
            pe.wait_ge(s_c, 32)
            pe.transpose(ps[:, 7, 0:2 * KD], csrc[0:2 * KD, :], ident[0:2 * KD, 0:2 * KD]).then_inc(s_ct, 1)
            pe.wait_ge(s_sc, 1)
            scv = scT.rearrange("p (v k) -> p k v", v=2)
            for l, n, i in ada_groups(pe):
                for s in range(NW):
                    if i is None:
                        pe.wait_ge(ada_w[s], 16)
                    else:
                        pe.wait_ge(ada_w[s], 4 * i + 16)
                        pe.wait_ge(ada_row, i + s - NW + 1)
                    for k in range(KD):
                        ins = mm(ps[0:2, s, :], scv[:, k, :], adaw[s][:, k, :], k == 0, k == KD - 1)
                    ins.then_inc(ada_mm, 1)
                if i is None:
                    pe.wait_ge(par_in, 16 * 8)
                    for k in range(KD):
                        pe.transpose(ps[:, 5, k * NPAR:(k + 1) * NPAR], psrc[0:NPAR, k * P:(k + 1) * P],
                                     ident[0:NPAR, 0:NPAR])
                    for k in range(KE):
                        ins = pe.transpose(ps[:, 6, 5 * k:5 * k + 5], psrc2[0:5, k * P:(k + 1) * P], ident[0:5, 0:5])
                    ins.then_inc(par_tr, 1)

            def to_channels(n, t, j):
                src = hall[:, t, :] if n in (1, 3) else CH[n]["h"][j % 2]
                pe.wait_ge(h_rdy, j + 1)
                if j:
                    pe.wait_ge(ht_rdy, j)
                for k in range(KD):
                    ins = pe.transpose(ps[:, 4 + k // 4, (k % 4) * P:(k % 4 + 1) * P], src[:, k * P:(k + 1) * P], ident)
                ins.then_inc(tr_rdy, 1)

            def route(n, t, j):
                pe.wait_ge(ht_rdy, j + 1)
                for k in range(KD):
                    ins = mm(ps[:, 6, t * NX:(t + 1) * NX], CH[n]["htt"][:, k, :], wrt[:, k, :], k == 0, k == KD - 1)
                ins.then_inc(lg_rdy, 1)

            def project(n, t, j, acts, w, kn):
                b0 = 2 * (j % 2)
                if j - 2 >= tiles_of(n)[0][1]:
                    pe.wait_ge(x_new, j - 1 - NT)
                for q in range(2):
                    for k in range(kn):
                        ins = mm(ps[:, b0 + q, :], acts(k, t), w[q][:, k, :], k == 0, k == kn - 1)
                ins.then_inc(y_mm, 1)

            def projected_chain(n, acts, w, kn):
                tl = tiles_of(n)
                for i in range(len(tl) + 2):
                    if i < len(tl):
                        project(n, *tl[i], acts, w, kn)
                    if 1 <= i <= len(tl):
                        to_channels(n, *tl[i - 1])
                        route(n, *tl[i - 1])

            def positions(l):
                pe.wait_ge(mk_rdy, l + 1)
                tl = [t for t, _ in tiles_of(1 + 2 * l)]
                for t in tl:
                    for u in [u for u in tl if u < t]:
                        mm(ps[:, 7, t * NX:(t + 1) * NX], ones[:], r_m[:, u, :], u == tl[0], False)
                    mm(ps[:, 7, t * NX:(t + 1) * NX], cst[:, C_TRI:C_TRI + P], r_m[:, t, :], t == tl[0], True)
                for u in tl:
                    ins = mm(ps[:, 7, P:P + NX], ones[:], r_m[:, u, :], u == tl[0], u == tl[-1])
                ins.then_inc(pos_rdy, 1)

            def turn_x():
                for k in range(KD):
                    ins = pe.transpose(ps[:, 4 + k // 4, (k % 4) * P:(k % 4 + 1) * P], xg[:, k * P:(k + 1) * P], ident)
                return ins

            def parts(bank, ah, al, slot, q, first, last):
                cols = slice(512 * q, 512 * q + 512)
                mm(bank, ah, wh[:, slot, cols], first, False)
                mm(bank, ah, wl[:, slot, cols], False, False)
                return mm(bank, al, wh[:, slot, cols], False, last)

            def experts(l):
                m = moe[l]
                pe.sem_inc(m["used"], 8)
                pe.wait_ge(m["xg"], 16)
                turn_x().then_inc(m["tx"], 1)
                nb = pe.value_load(table[0:1, 31:32], min_val=NX, max_val=NB - 1)
                with pe.Fori(0, nb) as b:
                    for kk in range(KD // 2):
                        pe.wait_ge(m["low"], made(b, "chunk", 4 * kk + 3))
                        for q in range(2):
                            for i in range(2):
                                k = 2 * kk + i
                                for mat in range(2):
                                    ins = parts(ps[:, 2 * q + mat, :], xTh[:, k, :], xTl[:, k, :],
                                                (4 * kk + 2 * mat + i) % NHL, q, k == 0, k == KD - 1)
                            if kk == KD // 2 - 1 and q == 0:
                                ins.then_inc(m["ab"], 1)
                        ins.then_inc(m["used"], 1)
                    pe.wait_ge(m["xg"], b * 16 + 32)
                    turn_x().then_inc(m["tx"], 1)
                    for q in range(2):
                        pe.wait_ge(m["g"], b * 2 + (q + 1))
                        for k in range(4):
                            ins = pe.transpose(ps[:, q, k * P:(k + 1) * P], gg[:, (4 * q + k) * P:(4 * q + k + 1) * P], ident)
                        ins.then_inc(m["tg"], 1)
                    pe.wait_ge(m["ye"], b + 1)
                    for kk in range(KD // 2):
                        if kk % 2 == 0:
                            pe.wait_ge(m["low"], made(b, "g", kk // 2))
                        if kk > 1:
                            pe.wait_ge(m["low"], made(b, "chunk", 2 * kk + 17))
                        for i in range(2):
                            k = 2 * kk + i
                            for q in range(2):
                                ins = parts(ps[:, 6 + q, :], gTh[:, k, :], gTl[:, k, :], k % NHL, q, k == 0, k == KD - 1)
                        ins.then_inc(m["used"], 1)

            pe.wait_ge(par_rdy, 1)
            for t, j in tiles_of(0):
                to_channels(0, t, j)
            pe.wait_ge(ht_rdy, NT)

            def wide(b0, lhs, rhs, kn):
                for k in range(kn):
                    mm(ps[:, b0, :], lhs(k), rhs(k)[:, 0:512], k == 0, k == kn - 1)
                    ins = mm(ps[:, b0 + 1, 0:S - 512], lhs(k), rhs(k)[:, 512:S], k == 0, k == kn - 1)
                return ins

            for ct in range(KD):
                g, o = ct // 2, (ct % 2) * P
                if ct % 2 == 0:
                    pe.wait_ge(abw[g % 2], 32 * (g // 2 + 1))
                if ct >= 2:
                    pe.wait_ge(glu_done, ct - 1)
                b0 = 4 * (ct % 2)
                for q in range(2):
                    ins = wide(b0 + 2 * q, lambda k: ring[g % 2][:, k, 256 * q + o:256 * q + o + P],
                               lambda k: hT[:, k, :], KD)
                ins.then_inc(ab_u, 1)
            pe.wait_ge(wp_in, 16)
            for p in range(KD + 4):
                if p < KD:
                    g, o = p // 4, (p % 4) * P
                    if p % 4 == 0:
                        pe.wait_ge(abw[g % 2], 64 + 16)
                    b0 = 2 * (p % 2)
                    if p == 0:
                        pe.wait_ge(glu_done, KD)
                    if p >= 2:
                        pe.wait_ge(bp_rdy, p - 1)
                    wide(b0, lambda k: ring[g][:, k, o:o + P], lambda k: hT[:, k, :], KD).then_inc(pl_u, 1)
                if p >= 4 and p % 2 == 1:
                    g = (p - 5) // 2
                    pe.wait_ge(pool_s, POOL_DONE[2 * g + 1])
                    for q in range(2):
                        if g:
                            pe.wait_ge(p_rdy, 2 * g - 1 + q)
                        wide(4 + 2 * q, lambda k: wpool[:, 2 * g + k, q * P:(q + 1) * P],
                             lambda k: pooled[(2 * g + k) % 4], 2).then_inc(pg_mm, 1)
            pe.wait_ge(bp_rdy, KD)
            for ct in range(KD):
                pe.wait_ge(conv_s, CONV_OPS * (ct + 1))
                for q, n in ((0, 512), (1, S - 512)):
                    ins = mm(ps[:, q, 0:n], onesd[:], catT[:, ct, 512 * q:512 * q + n], ct == 0, ct == KD - 1)
            ins.then_inc(ln_mu, 1)
            for ct in range(KD):
                pe.wait_ge(ln_sq, ct + 1)
                for q, n in ((0, 512), (1, S - 512)):
                    ins = mm(ps[:, 2 + q, 0:n], onesd[:], sg[ct % 2][:, 512 * q:512 * q + n], ct == 0, ct == KD - 1)
                ins.then_inc(ln_sm, 1)
            pe.wait_ge(ln_y, KD)
            pe.wait_ge(p_rdy, KD)
            for q in range(4):
                pe.wait_ge(wo_in[q], 16)
            pe.wait_ge(wr_in, 32)
            projected_chain(1, lambda k, t: catT[:, k, t * P:(t + 1) * P], wo, 2 * KD)
            positions(0)
            experts(0)
            for t, j in tiles_of(2):
                to_channels(2, t, j)
            pe.wait_ge(ht_rdy, 3 * NT)
            for ct in range(KE):
                g, o = ct // 4, (ct % 4) * P
                if ct % 4 == 0:
                    pe.wait_ge(cw[g % 2], 16 * (g // 2 + 1))
                if ct >= 4:
                    pe.wait_ge(cv_s, CV_OPS * (ct - 4) + 2)
                wide(2 * (ct % 4), lambda k: cring[g % 2][:, k, o:o + P], lambda k: hT[:, k, :], KD).then_inc(xm_mm, 1)
            for z in range(16):
                g, i = z // 4, z % 4
                if i == 0:
                    pe.wait_ge(cw[g % 2], 16 * (g // 2 + 3))
                if z < 8:
                    pe.wait_ge(cv_s, CV_OPS * (12 + z // 2) + 2)
                else:
                    pe.wait_ge(z_rdy, z - 7)
                for k in range(KD):
                    ins = mm(ps[:, z % 8, :], hT[:, k, S_CTX + i * P:S_CTX + (i + 1) * P], cring[g % 2][:, k, :],
                             k == 0, k == KD - 1)
                ins.then_inc(z_mm, 1)
            pe.wait_ge(bd_rdy, 3)
            pe.wait_ge(z_rdy, 16)
            pe.wait_ge(wp_in, 32)

            def turn_bd(bt):
                if bt >= 2:
                    pe.wait_ge(bt_ev, bt - 1)
                for i, (m_, t) in enumerate(BATCH[bt]):
                    ins = pe.transpose(ps[:, bt % 2, i * P:(i + 1) * P], BD[:, m_, t, :], ident)
                ins.then_inc(bt_mm, 1)

            turn_bd(0)
            for bt in range(12):
                if bt + 1 < 12:
                    turn_bd(bt + 1)
                pe.wait_ge(bt_ev, bt + 1)
                for i, (m_, t) in sorted(enumerate(BATCH[bt]), key=lambda e: (e[1][1], e[1][0])):
                    row = (t if m_ < 2 else KE + t) * NX
                    ins = mm(ps[:, 2, row:row + NX], bdt[bt % 2][:, i, :], wg[:, m_ * KE + t, :], m_ != 1, m_ != 0)
                if bt == 11:
                    ins.then_inc(ge_mm, 1)
                else:
                    ins.then_inc(ge_mm, 1)
            pe.wait_ge(ge_rdy, 4)
            for t in range(KE):
                pe.wait_ge(xc_rdy, t + 1)
                mm(ps[:, 4, 256:512], geff[:, t, :], xc[:, t, 0:S_CTX], t == 0, False)
                mm(ps[:, 5, :], geff[:, t, :], xc[:, t, S_CTX + 2:], t == 0, False)
            for t in range(KE):
                mm(ps[:, 4, 256:512], geff[:, KE + t, :], xm[:, t, 2:2 + S_CTX], False, t == KE - 1)
                ins = mm(ps[:, 5, :], geff[:, KE + t, :], xm[:, t, 4 + S_CTX:4 + S], False, t == KE - 1)
            ins.then_inc(g_mm, 1)
            for h in range(H):
                pe.wait_ge(gr, R_G) if h == 0 else pe.wait_ge(v_ev, 6 * h)
                for tt in range(NT):
                    o = 2 + tt * P if tt < CT else 4 + tt * P
                    for cc in range(HC):
                        t = h * HC + cc
                        ins = mm(ps[:, tt, cc * P:(cc + 1) * P], xm[:, t, o:o + P], BD[:, 2, t, :], True, True)
                ins.then_inc(v_mm, 1)
            pe.wait_ge(gr, R_M)
            pe.wait_ge(ga, A_FL)
            for i in range(4):
                o = S_CTX + i * P
                pe.transpose(ps[:, 6, 64 * i:64 * i + 64], r_M[0:64, o:o + P], ident[0:64, 0:64])
                ins = pe.transpose(ps[:, 7, 64 * i:64 * i + 64], r_fl[0:64, o:o + P], ident[0:64, 0:64])
            ins.then_inc(stt_mm, 1)
            pe.wait_ge(v_ev, 6 * H)
            pe.wait_ge(st_rdy, 2)
            for t in range(KE):
                b0 = 4 * (t % 2)
                if t >= 2:
                    pe.wait_ge(k_ev, 2 * (t - 1))
                    pe.wait_ge(q_ev, t - 1)
                mm(ps[:, b0, 256:512], BD[:, 1, t, :], xc[:, t, 0:S_CTX], True, True)
                mm(ps[:, b0 + 1, :], BD[:, 1, t, :], xc[:, t, S_CTX + 2:], True, True)
                mm(ps[:, b0 + 2, :], BD[:, 0, t, :], xc[:, t, S_CTX + 2:], True, True).then_inc(kq_mm, 1)
            pe.wait_ge(k_ev, 2 * KE)
            pe.wait_ge(q_ev, KE)

            def scores(u):
                h, i = u // 4, u % 4
                b0 = 2 * (u % 2)
                if u >= 2:
                    pe.wait_ge(aA, 4 * (u - 2) + 1)
                for cc in range(HC):
                    t = h * HC + cc
                    lhs = qT[:, t, i * P:(i + 1) * P]
                    mm(ps[:, b0, 256:512], lhs, xc[:, t, 0:S_CTX], cc == 0, cc == HC - 1)
                    ins = mm(ps[:, b0 + 1, :], lhs, xc[:, t, S_CTX + 2:], cc == 0, cc == HC - 1)
                ins.then_inc(sS, 1)

            def turn_y(u):
                pe.wait_ge(hV, u + 1)
                if u:
                    pe.wait_ge(yT_ev, u)
                for cc in range(HC):
                    ins = pe.transpose(ps[:, 7, cc * P:(cc + 1) * P], hv[:, cc * P:(cc + 1) * P], ident)
                ins.then_inc(yT_mm, 1)

            scores(0)
            for u in range(16):
                h, i = u // 4, u % 4
                if u + 1 < 16:
                    scores(u + 1)
                pe.wait_ge(aA, 4 * u + 4)
                if u:
                    pe.wait_ge(aT, u)
                for s in range(NT):
                    ins = pe.transpose(ps[:, 4 + s // 4, (s % 4) * P:(s % 4 + 1) * P], AA[u % 2][:, s * P:(s + 1) * P], ident)
                ins.then_inc(tT, 1)
                if u:
                    turn_y(u - 1)
                pe.wait_ge(aT, u + 1)
                for s in range(NT):
                    ins = mm(ps[:, 6, :], AT[:, s * P:(s + 1) * P], vv[h][:, s, :], s == 0, s == NT - 1)
                ins.then_inc(pV, 1)
            turn_y(15)
            pe.wait_ge(yT_ev, 16)
            for q in range(4):
                pe.wait_ge(wo_in[q], 32)
            projected_chain(3, lambda k, t: qT[:, k, (t - CT) * P:(t - CT + 1) * P], woc, KE)
            positions(1)
            experts(1)

        @block.scalar
        def _(act):
            def go(out_, in_, f, **kw):
                return act.activation(out_, in_, f, **kw)

            act.wait_ge(s_ct, 1)
            go(scT, ps[:, 7, 0:2 * KD], ACT.Silu).then_inc(s_sc, 1)
            for l, n, i in ada_groups(act):
                for s in range(NW):
                    act.wait_ge(ada_row, s + 1 if i is None else i + s + 1)
                    dst = mods_d[l, :, n * 512 + s * 512:n * 512 + s * 512 + 512] if i is None else \
                        mods_d[l, :, bass.ds(n * 512 + s * 512, 512)]
                    act.dma_start(dst, stage[s][0:2, :]).then_inc(ada_st[s], 16)
            for s in range(NW):
                act.wait_ge(ada_st[s], 16 * 2 * NA // NW)
            go(ss[:, 0:1], ones[:, 0:1], ACT.Copy).then_inc(ada_all, 1)

            def norm(n, t, j):
                s = j % 2
                dst = hall[:, t, :] if n in (1, 3) else CH[n]["h"][s]
                if n in (0,):
                    act.wait_ge(xt_in[s], 16 * (j // 2 + 1))
                else:
                    act.wait_ge(x_new, j + 1 - NT)
                if n in (0, 2) and j - 2 >= tiles_of(n)[0][1]:
                    act.wait_ge(tr_rdy, j - 1)
                if n == 4 and j - 2 >= tiles_of(n)[0][1]:
                    act.wait_ge(out_st[s], 16 * ((j - tiles_of(4)[0][1]) // 2))
                if j >= 2:
                    act.wait_ge(h_rdy, j - 1)
                go(dst, CH[n]["xt"][s], ACT.Square, accum_out=ss[:, s:s + 1]).then_inc(ss_rdy, 1)
                act.wait_ge(ss_rdy, j + 1)
                go(rt[:, s:s + 1], ss[:, s:s + 1], ACT.Sqrt, scale=1.0 / D, bias=epsc[:]).then_inc(rt_rdy, 1)

            def turned(n, t, j):
                act.wait_ge(tr_rdy, j + 1)
                if n in (1, 3):
                    if t > tiles_of(n)[0][0]:
                        act.wait_ge(lg_rdy, lg_before(n, t))
                    dst = CH[n]["htt"]
                else:
                    dst = hT[:, :, t * P:(t + 1) * P]
                go(dst, psf[:, 4 * 512:6 * 512].rearrange("p (k n) -> p k n", n=P), ACT.Copy).then_inc(ht_rdy, 1)

            def chain(n):
                tl = tiles_of(n)
                for i in range(len(tl) + 1):
                    if i < len(tl):
                        norm(n, *tl[i])
                    if i and n < 4:
                        turned(n, *tl[i - 1])
                if n in (1, 3):
                    l = n // 2
                    act.wait_ge(lg_rdy, lg_before(n, NT))
                    t0 = tl[0][0]
                    go(r_sc[:, t0:, :].rearrange("p t e -> p (t e)"), ps[:, 6, t0 * NX:NT * NX], ACT.Sigmoid).then_inc(sc_rdy, 1)

            def experts(l):
                m = moe[l]

                def high(b, r, ahead=0):
                    g = r // 2
                    if r % 2 == 0:
                        act.wait_ge(m["w"][g % 6], b * 32 + (ahead * 32 + 16 * (g // 6 + 1)))
                    if r >= 8:
                        act.wait_ge(m["used"], b * 8 + (8 + (r - 8) // 4 + 1))
                    else:
                        act.wait_ge(m["used"], b * 8 + (8 * ahead + 4 + r // 2 + 1))
                    go(wh[:, r % NHL, :], wx[:, g % 6, r % 2, :], ACT.Copy).then_inc(m["high"], 1)

                for s in range(2):
                    act.wait_ge(xt_st[s], 16 * stores(2 * l + 2, -1, s))
                act.wait_ge(m["tx"], 1)
                go(xTh.rearrange("p k n -> p (k n)"), psf[:, 4 * 512:6 * 512], ACT.Copy).then_inc(m["high"], 1)
                for r in range(4):
                    high(0, r)
                nb = act.value_load(table[0:1, 31:32], min_val=NX, max_val=NB - 1)
                with act.Fori(0, nb) as b:
                    for r in range(4, 20):
                        high(b, r)
                    for q in range(2):
                        act.wait_ge(m["ab"], b + 1) if q == 0 else act.wait_ge(m["used"], b * 8 + 12)
                        go(s0[:, 512 * q:512 * q + 512], ps[:, 2 * q, :], ACT.Silu).then_inc(m["si"], 1)
                    for q in range(2):
                        act.wait_ge(m["tg"], b * 2 + (q + 1))
                        go(gTh[:, 4 * q:4 * q + 4, :], ps[:, q, :].rearrange("p (k n) -> p k n", n=P),
                           ACT.Copy).then_inc(m["high"], 1)
                    act.wait_ge(m["tx"], b + 2)
                    go(xTh.rearrange("p k n -> p (k n)"), psf[:, 4 * 512:6 * 512], ACT.Copy).then_inc(m["high"], 1)
                    for r in range(20, 24):
                        high(b, r)
                    for r in range(4):
                        high(b, r, 1)
                act.wait_ge(m["yst"], nb * 16 + 16)
                act.wait_ge(m["xg"], nb * 16 + 16)
                act.wait_ge(m["low"], nb * PARTS + 5)
                go(ss[:, 0:1], ones[:, 0:1], ACT.Copy).then_inc(m["done"], 1)

            act.wait_ge(s_one, 3)
            chain(0)
            act.wait_ge(par_rdy, 3)
            for ct in range(KD):
                act.wait_ge(ab_u, ct + 1)
                if ct >= 2:
                    act.wait_ge(glu_done, ct - 1)
                b0 = 4 * (ct % 2) + 2
                go(sg[ct % 2], psf[:, b0 * 512:b0 * 512 + S], ACT.Sigmoid).then_inc(sg_rdy, 1)
            act.wait_ge(pad_z, 7)

            def pooled_out(i):
                act.wait_ge(pg_mm, i + 1)
                b0 = 4 + 2 * (i % 2)
                go(catT[:, KD + i, :], psf[:, b0 * 512:b0 * 512 + S], ACT.Identity,
                   scale=par[:, i, TAPS + 4:TAPS + 5], bias=pscb[:, i:i + 1]).then_inc(p_rdy, 1)

            for p in range(KD + 4):
                if p < KD:
                    act.wait_ge(pl_u, p + 1)
                    if p >= 2:
                        act.wait_ge(pool_s, POOL_DONE[p - 2])
                    b0 = 2 * (p % 2)
                    rows = psf[:, b0 * 512:b0 * 512 + S].rearrange("p (r w) -> p r w", w=GRID_W)
                    go(bpad[p % 2][:, :, PH:PH + GRID_W], rows[:, 0:CROWS], ACT.Copy)
                    go(lpad[p % 2][:, PH:PH + LROWS], rows[:, CROWS:], ACT.Copy).then_inc(bp_rdy, 1)
                if p >= 5 and p % 2 == 1:
                    pooled_out(p - 5)
                    pooled_out(p - 4)
            for ct in range(KD):
                act.wait_ge(ln_d, ct + 1)
                if ct >= 2:
                    act.wait_ge(ln_sm, ct - 1)
                go(sg[ct % 2], catT[:, ct, :], ACT.Square).then_inc(ln_sq, 1)
            act.wait_ge(ln_ve, 1)
            act.wait_ge(ln_sm, KD)
            go(sg[0], lnv, ACT.Sqrt).then_inc(ln_sd, 1)
            for ct in range(KD):
                act.wait_ge(ln_n, ct + 1)
                go(catT[:, ct, :], catT[:, ct, :], ACT.Silu, scale=par[:, ct, TAPS + 1:TAPS + 2],
                   bias=par[:, ct, TAPS + 2:TAPS + 3]).then_inc(ln_y, 1)
            chain(1)
            experts(0)
            chain(2)
            for ct in range(KE):
                act.wait_ge(cv_s, CV_OPS * (ct + 1))
                go(xc[:, ct, :], xc[:, ct, :], ACT.Silu).then_inc(xc_rdy, 1)
            for z in range(16):
                g, i = z // 4, z % 4
                act.wait_ge(z_mm, z + 1)
                if z >= 2:
                    act.wait_ge(z_st[z % 2], 16 * (z // 2))
                go(zst[z % 2], ps[:, z % 8, :], ACT.Sigmoid).then_inc(z_rdy, 1)
                act.wait_ge(z_rdy, z + 1)
                act.dma_start(zs_d[i * P:(i + 1) * P, g * 512:(g + 1) * 512], zst[z % 2]).then_inc(z_st[z % 2], 16)
            for bt in range(12):
                act.wait_ge(bt_mm, bt + 1)
                if bt >= 2:
                    act.wait_ge(ge_mm, bt - 1)
                go(bdt[bt % 2], ps[:, bt % 2, :].rearrange("p (a b) -> p a b", b=P), ACT.Copy).then_inc(bt_ev, 1)
            act.wait_ge(ge_mm, 12)
            act.wait_ge(xm_z, 4)
            pg = ps[:, 2, :].rearrange("p (t a h) -> p t a h", a=4, h=H)
            gv = geff.rearrange("p t (a n) -> p t a n", a=4)
            for i in range(4):
                go(gv[:, :, i, 0:H], pg[:, :, GATE_COL[i], :], ACT.Copy).then_inc(ge_rdy, 1)
            act.wait_ge(gr, R_F)
            act.wait_ge(ge_mm, 12)
            go(r_x[0:64, :], r_lf[0:64, :], ACT.Abs).then_inc(ga, 1)
            act.wait_ge(ga, 1)
            go(r_x[0:64, :], r_x[0:64, :], ACT.Exp, scale=-1.0).then_inc(ga, 1)
            act.wait_ge(ga, 2)
            go(r_x[0:64, :], r_x[0:64, :], ACT.Ln, bias=ones[0:64, 0:1]).then_inc(ga, 1)
            act.wait_ge(gr, R_X)
            go(r_fl[0:64, :], r_x[0:64, :], ACT.Exp, scale=-1.0).then_inc(ga, 1)
            for h in range(H):
                act.wait_ge(v_mm, h + 1)
                for tt in range(0, NT, 2):
                    go(vv[h][:, tt, :], ps[:, tt, :], ACT.Copy).then_inc(v_ev, 1)
            for t in range(KE):
                act.wait_ge(kq_mm, t + 1)
                b0 = 4 * (t % 2)
                go(xc[:, t, 0:S_CTX], ps[:, b0, 256:512], ACT.Copy).then_inc(k_ev, 1)
                go(xc[:, t, S_CTX + 2:], ps[:, b0 + 1, :], ACT.Copy).then_inc(k_ev, 1)
            act.wait_ge(st_rdy, 2)
            act.wait_ge(ab_in, 16)

            def exps(u):
                h, i = u // 4, u % 4
                o = S_CTX + i * P
                if u:
                    act.wait_ge(aA, 4 * u)
                f, b = st[:, 0, i, 0, h:h + 1], st[:, 0, i, 1, h:h + 1]
                go(Ef[:, 0:o], abc[:, h, 0:o], ACT.Exp, bias=f)
                go(Eb[:, 0:S_CTX], abc[:, H + h, 0:S_CTX], ACT.Exp, bias=b)
                if i < 3:
                    go(Eb[:, o + P:S], abc[:, H + h, o + P:S], ACT.Exp, bias=b)
                act.wait_ge(dg, 2 * u + 2)
                go(Ef[:, o:o + P], Ef[:, o:o + P], ACT.Exp, bias=f)
                go(Eb[:, o:o + P], Eb[:, o:o + P], ACT.Exp, bias=b).then_inc(eE, 1)

            def y_out(u):
                act.wait_ge(yT_mm, u + 1)
                h, i = u // 4, u % 4
                go(qT[:, h * HC:(h + 1) * HC, i * P:(i + 1) * P], ps[:, 7, :].rearrange("p (a b) -> p a b", b=P),
                   ACT.Copy).then_inc(yT_ev, 1)

            exps(0)
            for u in range(16):
                act.wait_ge(tT, u + 1)
                if u:
                    act.wait_ge(pV, u)
                go(AT, psf[:, 4 * 512:4 * 512 + S], ACT.Copy).then_inc(aT, 1)
                if u:
                    y_out(u - 1)
                if u + 1 < 16:
                    exps(u + 1)
                act.wait_ge(lV, u + 1)
                go(bst[:, u % 2, 8:9], bst[:, u % 2, 7:8], ACT.Ln, bias=epsc[:]).then_inc(lX, 1)
                act.wait_ge(lX, 2 * u + 1)
                go(bst[:, u % 2, 9:10], bst[:, u % 2, 8:9], ACT.Exp, scale=-0.5).then_inc(lX, 1)
            y_out(15)
            chain(3)
            experts(1)
            chain(4)

        @block.vector
        def _(v):
            n = [0]

            def link(ins):
                n[0] += 1
                ins.then_inc(dv, 1)
                v.wait_ge(dv, n[0])

            v.memset(ones[:], 1.0).then_inc(s_one, 1)
            v.memset(onesd[:], 1.0 / D).then_inc(s_one, 1)
            v.memset(epsc[:], EPS).then_inc(s_one, 1)
            link(v.memset(gbias[:], 0.0))
            v.wait_ge(s_bada, 32)
            for l, nn, i in ada_groups(v):
                for s in range(NW):
                    if i is None:
                        v.wait_ge(ada_mm, s + 1)
                        col = bada[0:2, s * 512:s * 512 + 512]
                    else:
                        v.wait_ge(ada_mm, i + s + 1)
                        v.wait_ge(ada_st[s], 4 * i)
                        col = bada[0:2, bass.ds(i * 512 + s * 512, 512)]
                    v.tensor_tensor(stage[s][0:2, :], ps[0:2, s, :], col, ALU.add).then_inc(ada_row, 1)
                if i is None:
                    v.wait_ge(par_tr, 1)
                    v.tensor_copy(par[:].rearrange("p k n -> p (k n)"), ps[:, 5, 0:KD * NPAR]).then_inc(par_rdy, 1)
                    v.tensor_copy(par2[:].rearrange("p k n -> p (k n)"), ps[:, 6, 0:5 * KE]).then_inc(par_rdy, 1)
                    v.wait_ge(par_rdy, 2)
                    v.tensor_tensor(pscb[:], par[:, :, TAPS + 3], par[:, :, TAPS + 4], ALU.mult).then_inc(par_rdy, 1)

            def chain(nn):
                ch = CH[nn]
                m, tmp = ch["mod"], ch["tmp"]
                v.wait_ge(s_mod, MODS[nn])
                if nn < 4:
                    for o in ((3,) if nn == 3 else (0, 3)):
                        link(v.scalar_tensor_tensor(m[o], m[o], 1.0, tmp, ALU.add, ALU.mult))
                for t, j in tiles_of(nn):
                    s = j % 2
                    o = 0 if t < CT else 3
                    xt = ch["xt"][s]
                    v.wait_ge(xt_in[s], 16 * (j // 2 + 1))
                    if nn in (1, 3):
                        v.wait_ge(y_mm, y_before(nn, t) + 1)
                        b0 = 2 * s * 512
                        link(v.tensor_tensor(tmp, psf[:, b0:b0 + D], m[o + 2], ALU.mult))
                        v.tensor_tensor(xt, xt, tmp, ALU.add).then_inc(x_new, 1)
                        v.wait_ge(x_new, j + 1 - NT)
                    if nn in (2, 4):
                        v.wait_ge(y_in[s], 32 * y_gathered(nn, j))
                        ya, yb = ch["y"][0][s], ch["y"][1][s]
                        link(v.tensor_scalar(ya, ya, wsel[:, 0, t:t + 1], None, ALU.mult))
                        link(v.scalar_tensor_tensor(ya, yb, wsel[:, 1, t:t + 1], ya, ALU.mult, ALU.add))
                        link(v.tensor_tensor(ya, ya, m[o + 2], ALU.mult))
                        v.tensor_tensor(xt, xt, ya, ALU.add).then_inc(x_new, 1)
                        v.wait_ge(x_new, j + 1 - NT)
                    v.wait_ge(rt_rdy, j + 1)
                    link(v.reciprocal(rs[:, s:s + 1], rt[:, s:s + 1]))
                    dst = hall[:, t, :] if nn in (1, 3) else ch["h"][s]
                    if nn == 4:
                        v.scalar_tensor_tensor(dst, xt, rs[:, s:s + 1], tmp, ALU.mult, ALU.mult).then_inc(h_rdy, 1)
                    else:
                        link(v.scalar_tensor_tensor(dst, xt, rs[:, s:s + 1], m[o], ALU.mult, ALU.mult))
                        v.tensor_tensor(dst, dst, m[o + 1], ALU.add).then_inc(h_rdy, 1)

            def router(l):
                t0 = 0 if l == 0 else CT
                T = NT - t0

                def tv(a):
                    return a[:, t0:, :]

                def tf(a):
                    return tv(a).rearrange("p t e -> p (t e)")

                def tg(a):
                    return tf(a).rearrange("p (g e) -> p g e", e=4)

                TG = T * 4
                v.wait_ge(sc_rdy, l + 1)
                link(v.tensor_tensor(tv(r_bi), tv(r_sc), bc(brow[:], 1, T), ALU.add))
                tie = bc(cst[:, C_TIE:C_TIE + 16].rearrange("p (i j) -> p i j", j=4), 1, TG)

                def rank(dst, a, n_, tie_):
                    x1 = r_big[:, 0:n_ * 16].rearrange("p (g i j) -> p g i j", i=4, j=4)
                    x2 = r_big2[:, 0:n_ * 16].rearrange("p (g i j) -> p g i j", i=4, j=4)
                    v.tensor_tensor(x1, bc(a, 2, 4), bc(a, 3, 4), ALU.is_gt)
                    link(v.tensor_tensor(x2, bc(a, 2, 4), bc(a, 3, 4), ALU.is_equal))
                    link(v.tensor_tensor(x2, x2, tie_, ALU.mult))
                    link(v.tensor_tensor(x1, x1, x2, ALU.add))
                    link(v.tensor_reduce(dst, x1, AX.X, ALU.add))

                rank(tg(r_t), tg(r_bi), TG, tie)
                link(v.tensor_scalar(tf(r_t), tf(r_t), 2.0, None, ALU.is_lt))
                link(v.tensor_tensor(tf(r_f), tf(r_bi), tf(r_t), ALU.mult))
                gs = r_s[:, 0:TG]
                link(v.tensor_reduce(gs, tg(r_f), AX.X, ALU.add))
                gr_ = r_s[:, 24:24 + TG]
                rank(gr_.rearrange("p (t g) -> p t g", g=4), gs.rearrange("p (t g) -> p t g", g=4), T,
                     bc(cst[:, C_TIE:C_TIE + 16].rearrange("p (i j) -> p i j", j=4), 1, T))
                link(v.tensor_scalar(gr_, gr_, 1.0, None, ALU.is_lt))
                v.tensor_tensor(tg(r_m), tg(r_t), bc(gr_, 2, 4), ALU.mult).then_inc(mk_rdy, 1)
                v.wait_ge(mk_rdy, l + 1)
                link(v.tensor_tensor(tf(r_w), tf(r_sc), tf(r_m), ALU.mult))
                sw = r_s[:, 48:48 + T]
                link(v.tensor_reduce(sw, tv(r_w), AX.X, ALU.add))
                link(v.reciprocal(sw, sw))
                link(v.tensor_tensor(tv(r_w), tv(r_w), bc(sw, 2, NX), ALU.mult))
                v.wait_ge(pos_rdy, l + 1)
                link(v.tensor_copy(tf(r_pos), ps[:, 7, t0 * NX:NT * NX]))
                cnt = r_s[:, 56:72]
                link(v.tensor_copy(cnt, ps[:, 7, P:P + NX]))
                th = cst[:, C_TH:C_TH + FMAX]
                big = r_big[:, 0:NX * FMAX].rearrange("p (e f) -> p e f", f=FMAX)
                link(v.tensor_tensor(big, bc(cnt, 2, FMAX), bc(th, 1, NX), ALU.is_gt))
                ov, cum, ovs = r_s[:, 72:88], r_s[:, 88:104], r_s[:, 104:120]
                link(v.tensor_reduce(ov, big, AX.X, ALU.add))
                link(v.tensor_tensor_scan(cum, ones[:, 0:NX], ov, 0.0, ALU.mult, ALU.add))
                link(v.tensor_tensor(ovs, cum, ov, ALU.subtract))
                big = r_big[:, 0:T * NX * FMAX].rearrange("p (e f) -> p e f", f=FMAX)
                link(v.tensor_tensor(big, bc(tf(r_pos), 2, FMAX), bc(th, 1, T * NX), ALU.is_ge))
                link(v.tensor_reduce(tf(r_f), big, AX.X, ALU.add))
                e_row = cst[:, C_E:C_E + NX]
                d_ = r_s[:, 120:136]
                link(v.scalar_tensor_tensor(d_, ovs, NX - 1.0, e_row, ALU.add, ALU.subtract))
                link(v.tensor_tensor(tv(r_sl), tv(r_f), bc(d_, 1, T), ALU.add))
                link(v.tensor_scalar(tf(r_t), tf(r_f), 1.0, None, ALU.min))
                link(v.tensor_tensor(tf(r_sl), tf(r_sl), tf(r_t), ALU.mult))
                link(v.tensor_tensor(tv(r_sl), tv(r_sl), bc(e_row, 1, T), ALU.add))
                link(v.scalar_tensor_tensor(tf(r_pos), tf(r_f), -float(P), tf(r_pos), ALU.mult, ALU.add))
                link(v.scalar_tensor_tensor(tf(r_sl), tf(r_pos), float(NB), tf(r_sl), ALU.mult, ALU.add))
                link(v.scalar_tensor_tensor(tf(r_sl), tf(r_sl), 1.0, tf(r_m), ALU.add, ALU.mult))
                link(v.tensor_scalar(tf(r_t), tf(r_m), -BIG, BIG, ALU.mult, ALU.add))
                link(v.tensor_tensor(tf(r_t), tf(r_t), tf(r_sl), ALU.add))
                sk = r_s[:, 136:136 + 2 * NT].rearrange("p (k t) -> p k t", k=2)
                link(v.tensor_reduce(sk[:, 0, t0:], tv(r_sl), AX.X, ALU.max))
                link(v.tensor_reduce(sk[:, 1, t0:], tv(r_t), AX.X, ALU.min))
                for k in range(2):
                    link(v.tensor_tensor(tv(r_f), tv(r_sl), bc(sk[:, k, t0:], 2, NX), ALU.is_equal))
                    link(v.tensor_tensor(tf(r_f), tf(r_f), tf(r_w), ALU.mult))
                    link(v.tensor_reduce(wsel[:, k, t0:], tv(r_f), AX.X, ALU.add))
                link(v.tensor_scalar(slots[:, :, t0:], sk[:, :, t0:], -1.0, None, ALU.add))
                tb = r_s[0:1, 160:192]
                j_row = cst[0:1, C_J:C_J + NB - NX]
                tbig = r_big[0:1, 0:(NB - NX) * NX].rearrange("p (j e) -> p j e", e=NX)
                link(v.tensor_tensor(tbig, bc(cum[0:1, :], 1, NB - NX), bc(j_row, 2, NX), ALU.is_le))
                link(v.memset(tb, 0.0))
                link(v.tensor_reduce(tb[:, NX:NB], tbig, AX.X, ALU.add))
                link(v.tensor_scalar(tb[:, NX:NB], tb[:, NX:NB], NX - 1.0, None, ALU.min))
                link(v.tensor_copy(tb[:, 0:NX], e_row[0:1, :]))
                link(v.tensor_scalar(tb[:, 31:32], cum[0:1, NX - 1:NX], float(NX), None, ALU.add))
                v.tensor_copy(table[:], tb).then_inc(sl_rdy, 1)

            def experts(l):
                m = moe[l]

                def low(b, r, ahead=0):
                    v.wait_ge(m["high"], made(b, "chunk", r, PARTS * ahead))
                    v.tensor_tensor(wl[:, r % NHL, :], wx[:, r // 2 % 6, r % 2, :], wh[:, r % NHL, :].bitcast(F32),
                                    ALU.subtract).then_inc(m["low"], 1)

                def low_x():
                    v.tensor_tensor(xTl.rearrange("p k n -> p (k n)"), psf[:, 4 * 512:6 * 512],
                                    xTh.rearrange("p k n -> p (k n)").bitcast(F32), ALU.subtract).then_inc(m["low"], 1)

                v.wait_ge(m["high"], 1)
                low_x()
                for r in range(4):
                    low(None, r)
                v.memset(yy, 0.0).then_inc(m["ye"], 1)
                nb = v.value_load(table[0:1, 31:32], min_val=NX, max_val=NB - 1)
                with v.Fori(0, nb) as b:
                    for r in range(4, 20):
                        low(b, r)
                    for q in range(2):
                        v.wait_ge(m["si"], b * 2 + (q + 1))
                        v.tensor_tensor(gg[:, 512 * q:512 * q + 512], s0[:, 512 * q:512 * q + 512],
                                        ps[:, 2 * q + 1, :], ALU.mult).then_inc(m["g"], 1)
                    for q in range(2):
                        v.wait_ge(m["high"], made(b, "g", q))
                        v.tensor_tensor(gTl[:, 4 * q:4 * q + 4, :], ps[:, q, :].rearrange("p (k n) -> p k n", n=P),
                                        gTh[:, 4 * q:4 * q + 4, :].bitcast(F32), ALU.subtract).then_inc(m["low"], 1)
                    v.wait_ge(m["high"], made(b, "x", 0, PARTS - 4))
                    low_x()
                    for r in range(20, 24):
                        low(b, r)
                    for r in range(4):
                        low(b, r, 1)
                    v.wait_ge(m["used"], b * 8 + 16)
                    v.wait_ge(m["yst"], b * 16 + 16)
                    v.tensor_copy(yy, psf[:, 6 * 512:8 * 512]).then_inc(m["ye"], 1)

            chain(0)
            v.wait_ge(pad_z, 7)
            for ct in range(KD):
                ap = apad[ct % 2]
                b0 = 4 * (ct % 2)
                v.wait_ge(sg_rdy, ct + 1)
                if ct:
                    v.wait_ge(conv_s, CONV_OPS * ct)
                v.tensor_tensor(ap[:, :, HALO:HALO + GRID_W], psf[:, b0 * 512:b0 * 512 + S].rearrange("p (r w) -> p r w", w=GRID_W),
                                sg[ct % 2].rearrange("p (r w) -> p r w", w=GRID_W), ALU.mult).then_inc(glu_done, 1)
                v.wait_ge(glu_done, ct + 1)
                v.tensor_copy(ap[:, 0:CROWS - 1, HALO + GRID_W:RW], ap[:, 1:CROWS, HALO:2 * HALO]).then_inc(conv_s, 1)
                v.tensor_copy(ap[:, 1:CROWS, 0:HALO], ap[:, 0:CROWS - 1, GRID_W:GRID_W + HALO]).then_inc(conv_s, 1)
                acc = [catT[:, ct, :].rearrange("p (r w) -> p r w", w=GRID_W), acc1.rearrange("p (r w) -> p r w", w=GRID_W)]
                for k in range(TAPS):
                    src, w = ap[:, :, k:k + GRID_W], par[:, ct, k:k + 1]
                    v.wait_ge(conv_s, CONV_OPS * ct + (2 if k < 2 else k + 1))
                    if k == 0:
                        ins = v.tensor_scalar(acc[0], src, w, par[:, ct, TAPS:TAPS + 1], ALU.mult, ALU.add)
                    elif k == 1:
                        ins = v.tensor_scalar(acc[1], src, w, None, ALU.mult)
                    else:
                        ins = v.scalar_tensor_tensor(acc[k % 2], src, w, acc[k % 2], ALU.mult, ALU.add)
                    ins.then_inc(conv_s, 1)
                v.wait_ge(conv_s, CONV_OPS * ct + 2 + TAPS)
                v.tensor_tensor(acc[0], acc[0], acc[1], ALU.add).then_inc(conv_s, 1)
            v.wait_ge(ln_mu, 1)
            for ct in range(KD):
                v.tensor_tensor(catT[:, ct, :], catT[:, ct, :], psf[:, 0:S], ALU.subtract).then_inc(ln_d, 1)
            v.wait_ge(ln_sm, KD)
            v.tensor_scalar(lnv, psf[:, 2 * 512:2 * 512 + S], EPS, None, ALU.add).then_inc(ln_ve, 1)
            v.wait_ge(ln_sd, 1)
            link(v.reciprocal(sg[1], sg[0]))
            for ct in range(KD):
                v.tensor_tensor(catT[:, ct, :], catT[:, ct, :], sg[1], ALU.mult).then_inc(ln_n, 1)
            chain(1)
            router(0)
            experts(0)
            chain(2)
            v.wait_ge(xm_z, 3)
            for ct in range(KE):
                b0 = 2 * (ct % 4) * 512
                v.wait_ge(xm_mm, ct + 1)
                v.tensor_copy(xm[:, ct, 2:2 + S_CTX], psf[:, b0:b0 + S_CTX]).then_inc(cv_s, 1)
                v.tensor_copy(xm[:, ct, 4 + S_CTX:4 + S], psf[:, b0 + S_CTX:b0 + S]).then_inc(cv_s, 1)
                for k in range(4):
                    src = xm[:, ct, k:k + XC]
                    v.wait_ge(cv_s, CV_OPS * ct + 2 + k)
                    if k == 0:
                        ins = v.tensor_scalar(xc[:, ct, :], src, par2[:, ct, 0:1], par2[:, ct, 4:5], ALU.mult, ALU.add)
                    else:
                        ins = v.scalar_tensor_tensor(xc[:, ct, :], src, par2[:, ct, k:k + 1], xc[:, ct, :], ALU.mult, ALU.add)
                    ins.then_inc(cv_s, 1)
            g_n = [0]

            def row(ins):
                g_n[0] += 1
                ins.then_inc(gr, 1)
                v.wait_ge(gr, g_n[0])

            v.wait_ge(raw_in, 48 + 64)
            v.wait_ge(g_mm, 1)
            row(v.tensor_scalar(G, psf[:, 4 * 512 + 256:6 * 512], gbias[:], None, ALU.add))
            assert g_n[0] == R_G
            row(v.tensor_copy(r_lf[0:64, :], G[64:128, :]))
            assert g_n[0] == R_F
            row(v.memset(r_zero[0:64, :], 0.0))
            v.wait_ge(ga, 3)
            row(v.scalar_tensor_tensor(r_lf[0:64, :], r_lf[0:64, :], 0.0, r_x[0:64, :], ALU.min, ALU.subtract))
            row(v.memset(r_x[0:64, :], 1.0))

            def back(a, lo, hi):
                return a[32:36, lo:hi][:, ::-1]

            def scans(dst, d0, d1, op0, op1):
                row(v.tensor_tensor_scan(dst[0:4, :], d0[0:4, :], d1[0:4, :], 0.0, op0, op1))
                row(v.tensor_tensor_scan(back(dst, 0, S_CTX), back(d0, 0, S_CTX), back(d1, 0, S_CTX), 0.0, op0, op1))
                row(v.tensor_tensor_scan(back(dst, S_CTX, S), back(d0, S_CTX, S), back(d1, S_CTX, S),
                                         dst[32:36, 0:1], op0, op1))

            row(v.memset(r_b[0:64, :], 0.0))
            scans(r_b, r_x, r_lf, ALU.mult, ALU.add)
            row(v.tensor_tensor(r_a[0:64, :], G[0:64, :], r_b[0:64, :], ALU.subtract))
            assert g_n[0] == R_A, g_n
            row(v.memset(r_M[0:64, :], 0.0))
            scans(r_M, r_zero, r_a, ALU.add, ALU.max)
            row(v.tensor_tensor(r_x[0:64, :], r_b[0:64, :], r_M[0:64, :], ALU.add))
            assert g_n[0] == R_X, g_n
            row(v.tensor_scalar(r_M[0:64, :], r_M[0:64, :], -1.0, None, ALU.mult))
            assert g_n[0] == R_M, g_n
            for h in range(H):
                v.wait_ge(v_mm, h + 1)
                for tt in range(1, NT, 2):
                    v.tensor_copy(vv[h][:, tt, :], ps[:, tt, :]).then_inc(v_ev, 1)
            v.wait_ge(stt_mm, 1)
            for kind in range(2):
                v.tensor_copy(st[:, kind], ps[:, 6 + kind, 0:256].rearrange("p (i d r) -> p i d r", i=4, d=2)[:, :, :, 0:H]
                              ).then_inc(st_rdy, 1)
            v.wait_ge(ar_st, 32)
            for t in range(KE):
                v.wait_ge(kq_mm, t + 1)
                v.tensor_copy(qT[:, t, :], ps[:, 4 * (t % 2) + 2, :]).then_inc(q_ev, 1)
            scale = DH ** -0.5

            def weigh(u):
                h, i = u // 4, u % 4
                o = S_CTX + i * P
                sc_ = psf[:, 2 * (u % 2) * 512 + 256:2 * (u % 2) * 512 + 1024]
                d = dn[:, u % 2]
                A = AA[u % 2]
                v.wait_ge(sS, u + 1)
                v.wait_ge(eE, u + 1)
                if u >= 2:
                    v.wait_ge(tT, u - 1)
                v.scalar_tensor_tensor(Ef[:, 0:o + P], sc_[:, 0:o + P], scale, Ef[:, 0:o + P], ALU.mult, ALU.mult,
                                       accum_out=d[:, 0:1])
                v.scalar_tensor_tensor(Eb[:, 0:S_CTX], sc_[:, 0:S_CTX], scale, Eb[:, 0:S_CTX], ALU.mult, ALU.mult,
                                       accum_out=d[:, 1:2])
                v.scalar_tensor_tensor(Eb[:, o:S], sc_[:, o:S], scale, Eb[:, o:S], ALU.mult, ALU.mult,
                                       accum_out=d[:, 2:3]).then_inc(aA, 1)
                v.wait_ge(aA, 4 * u + 1)
                link(v.tensor_tensor(d[:, 1:2], d[:, 1:2], d[:, 2:3], ALU.add))
                link(v.scalar_tensor_tensor(d[:, 4:6], d[:, 0:2], -1.0, d[:, 0:2], ALU.mult, ALU.max))
                link(v.tensor_tensor(d[:, 4:6], d[:, 4:6], st[:, 1, i, :, h], ALU.max))
                link(v.reciprocal(d[:, 6:8], d[:, 4:6]))
                v.tensor_scalar(A[:, 0:o + P], Ef[:, 0:o + P], d[:, 6:7], None, ALU.mult).then_inc(aA, 1)
                v.wait_ge(aA, 4 * u + 2)
                if i < 3:
                    v.tensor_scalar(A[:, o + P:S], Eb[:, o + P:S], d[:, 7:8], None, ALU.mult)
                v.scalar_tensor_tensor(A[:, 0:S_CTX], Eb[:, 0:S_CTX], d[:, 7:8], A[:, 0:S_CTX], ALU.mult, ALU.add
                                       ).then_inc(aA, 1)
                v.scalar_tensor_tensor(A[:, o:o + P], Eb[:, o:o + P], d[:, 7:8], A[:, o:o + P], ALU.mult, ALU.add
                                       ).then_inc(aA, 1)

            def head_norm(u):
                h, i = u // 4, u % 4
                bs = bst[:, u % 2]
                v.wait_ge(pV, u + 1)
                link(v.bn_stats(bs[:, 0:6], ps[:, 6, :]))
                v.bn_aggr(bs[:, 6:8], bs[:, 0:6]).then_inc(lV, 1)
                v.wait_ge(lX, 2 * u + 2)
                if u:
                    v.wait_ge(yT_mm, u)
                link(v.tensor_scalar(hv, ps[:, 6, :], bs[:, 6:7], bs[:, 9:10], ALU.subtract, ALU.mult))
                v.wait_ge(hn_in, 16 * (h + 1))
                link(v.tensor_tensor(hv, hv, hn, ALU.mult))
                v.wait_ge(zl_in[u % 2], 16 * (u // 2 + 1))
                v.tensor_tensor(hv, hv, zl[u % 2], ALU.mult).then_inc(hV, 1)

            for s in range(2):
                v.wait_ge(z_st[s], 16 * 8)
            weigh(0)
            for u in range(16):
                if u + 1 < 16:
                    weigh(u + 1)
                head_norm(u)
            chain(3)
            router(1)
            experts(1)
            chain(4)


def lg_before(n, t):
    return t if n == 1 else NT + t - CT


def y_before(n, t):
    return lg_before(n, t)


def made(b, what, i, shift=0):
    n = {"x": 1, "chunk": i + 2 if i < 20 else i + 5, "g": 22 + i}[what] + shift
    return n if b is None else b * PARTS + n


def y_gathered(n, j):
    return sum(1 for m, t, i in CHAINS if m in (2, 4) and i <= j and i % 2 == j % 2)


AR = 51200
NW = 4
PARTS = 3 * KD + 3
NHL = 8
CONV_OPS = 2 + TAPS + 1
CV_OPS = 6
GATE_COL = (0, 2, 1, 3)
R_G, R_F, R_A, R_X, R_M = 1, 2, 10, 15, 16
A_FL = 4
POOL_DONE = []
for _p in range(KD):
    POOL_DONE.append((POOL_DONE[-1] if _p else 0) + 2 + 2 * (_p // 2 + 1) + 4)
BATCH = [[(m_, t + i) for m_ in (0, 1) for i in range(2)] for t in range(0, KE, 2)] + \
        [[(2, t + i) for i in range(4)] for t in range(0, KE, 4)]

_INS = ['x', 'c', 'ctx', 'c_ctx', 'w_ada', 'b_ada', 'g_mix', 'g_ffn', 'g_final', 'w_in_ab', 'w_dw_a', 'b_dw_a', 'ln_g_a',
        'ln_b_a', 'w_pool', 'b_pool', 'pool_scale', 'w_out_ab', 'w_in_c', 'w_conv_c', 'b_conv_c', 'w_q', 'w_k', 'w_v',
        'w_gates', 'b_gates', 'hn_g', 'w_out_c', 'w_router', 'b_router', 'w1', 'w3', 'w2']


def kernel(**inputs):
    import numpy as _np
    import concourse.bacc as _bacc
    from concourse import mybir as _mybir
    from concourse.bass_utils import run_bass_kernel_spmd as _run

    nc = _bacc.Bacc("TRN2", target_bir_lowering=False, num_devices=1)
    arrays, args = {}, []
    consts, rcounts = constants()
    for name in _INS + ["consts", "rcounts"]:
        a = _np.ascontiguousarray({"consts": consts, "rcounts": rcounts}[name] if name in ("consts", "rcounts") else inputs[name])
        arrays[f"in_{name}_dram"] = a
        args.append(nc.dram_tensor(f"in_{name}_dram", a.shape, _mybir.dt.from_np(a.dtype), kind="ExternalInput").ap())
    args.append(nc.dram_tensor("out_0_dram", (1, S_LAT, D), _mybir.dt.float32, kind="ExternalOutput").ap())
    program(nc, *args)
    r = _run(nc, [arrays], core_ids=[0])
    return r.results[0]["out_0_dram"]
```

```python
from contextlib import ExitStack

import numpy as np
import concourse.bass as bass
from concourse import mybir

F32 = mybir.dt.float32
F32R = mybir.dt.float32r
I32 = mybir.dt.int32
ALU = mybir.AluOpType
ACT = mybir.ActivationFunctionType
AX = mybir.AxisListType

P = 128
D = 1024
KD = D // P
S_CTX, S_LAT = 256, 512
S = S_CTX + S_LAT
NT = S // P
CT = S_CTX // P
E2 = 2 * D
KE = E2 // P
H, DH = 4, 512
HC = DH // P
GRID_W = 64
ROWS = S // GRID_W
CROWS = S_CTX // GRID_W
LROWS = ROWS - CROWS
RC = S_CTX + LROWS
TAPS, HALO = 31, 15
RW = GRID_W + 2 * HALO
PH = 8
PW = GRID_W + 2 * PH
WINDOWS = (2, 4, 8, 16)
NPAR = TAPS + 5
NX = 16
A_MAX = 2 * S
EXTRA = (A_MAX - 1) // P
NB = NX + EXTRA + 1
FMAX = S // P - 1
EPS = 1e-6
NEG = -1e30
BIG = 65536.0
XC = S + 2
XM = S + 5

CHAINS = []
for _n, _tiles in enumerate((range(NT), range(NT), range(NT), range(CT, NT), range(CT, NT))):
    for _t in _tiles:
        CHAINS.append((_n, _t, len(CHAINS)))


def tiles_of(n):
    return [(t, j) for m, t, j in CHAINS if m == n]


C_ID, C_TRI, C_NF, C_NB_, C_G4 = 0, 128, 256, 384, 512
C_TIE, C_E, C_J, C_TH = 544, 560, 576, 592
C_END = 600


def constants():
    c = np.zeros((P, C_END), np.float32)
    i = np.arange(P)
    c[:, C_ID:C_ID + P] = np.eye(P)
    c[:, C_TRI:C_TRI + P] = i[:, None] < i[None, :]
    c[:, C_NF:C_NF + P] = np.where(i[None, :] <= i[:, None], 0.0, NEG)
    c[:, C_NB_:C_NB_ + P] = np.where(i[None, :] >= i[:, None], 0.0, NEG)
    c[:, C_G4:C_G4 + 32] = np.arange(32)[None, :] == (i // 4)[:, None]
    c[:, C_TIE:C_TIE + 16] = (np.arange(4)[None, :] < np.arange(4)[:, None]).reshape(1, 16)
    c[:, C_E:C_E + NX] = np.arange(NX)
    c[:, C_J:C_J + 16] = np.arange(16)
    c[:, C_TH:C_TH + FMAX] = P * (1 + np.arange(FMAX))
    rc = np.zeros((4, RC), np.float32)
    for w_i, w in enumerate(WINDOWS):
        left, right = w // 2, w - 1 - w // 2
        for base, total, length in ((0, S_CTX, S_CTX), (S_CTX, LROWS, LROWS)):
            pos = np.arange(total)
            rc[w_i, base:base + total] = 1.0 / (np.minimum(pos + right + 1, length) - np.maximum(pos - left, 0))
    return c, rc.reshape(1, -1)


def bc(ap, axis, n):
    a = ap.unsqueeze(axis)
    shape = list(a.shape)
    shape[axis] = n
    return a.broadcast_to(shape)



def program(nc, x, c, ctx_in, c_ctx, w_ada, b_ada, g_mix, g_ffn, g_final, w_in_ab, w_dw_a, b_dw_a, ln_g_a, ln_b_a,
            w_pool, b_pool, pool_scale, w_out_ab, w_in_c, w_conv_c, b_conv_c, w_q, w_k, w_v, w_gates, b_gates,
            hn_g, w_out_c, w_router, b_router, w1, w3, w2, consts, rcounts, out):
    def dram(name, shape):
        return nc.dram_tensor(name, shape, F32, kind="Internal").ap()

    mods_d = dram("mods_d", [2, 2, 6 * D])
    xs_d = [None] + [dram(f"xs{n}_d", [S, D]) for n in (1, 2, 3)]
    buf_d = dram("buf_d", [P * NB, D])
    zs_d = dram("zs_d", [S_LAT, E2])
    arow_d = dram("arow_d", [2 * H, S])
    buf_v = buf_d.rearrange("(p b) d -> p b d", b=NB)

    es = ExitStack()
    with es:
        def sb(name, shape, dt=F32):
            return es.enter_context(nc.sbuf_tensor(name, shape, dt))

        def sem(name):
            return es.enter_context(nc.semaphore(name))

        def sems(names):
            return [sem(s) for s in names.split()]

        base = 0
        while base < nc.sbuf_base:
            base += 64
        arena = nc.alloc_sbuf_tensor_at("arena", [P, AR], F32, offset=base)
        fence = sb("fence", [P, AR + 16])
        cst = sb("cst", [P, C_END])
        ones = sb("ones", [P, P])
        onesd = sb("onesd", [P, P])
        par = sb("par", [P, KD, NPAR])
        pscb = sb("pscb", [P, KD])
        par2 = sb("par2", [P, KE, 5])
        gbias = sb("gbias", [P, 1])
        epsc = sb("epsc", [P, 1])
        ss = sb("ss", [P, 2])
        rt = sb("rt", [P, 2])
        rs = sb("rs", [P, 2])
        wrt = sb("wrt", [P, KD, NX])
        brow = sb("brow", [P, NX])
        slots = sb("slots", [P, 2, NT], I32)
        wsel = sb("wsel", [P, 2, NT])
        table = sb("table", [1, 32], I32)
        st = sb("st", [P, 2, 4, 2, H])
        dn = sb("dn", [P, 2, 16])
        bst = sb("bst", [P, 2, 16])
        ps = es.enter_context(nc.psum_tensor("ps", [P, 8, 512], F32))
        psf = ps[:].rearrange("p b n -> p (b n)")

        def at(off, *dims):
            n = int(np.prod(dims))
            a = arena[:, off:off + n]
            assert off + n <= AR, (off, dims)
            if len(dims) == 2:
                a = a.rearrange("p (a b) -> p a b", a=dims[0])
            if len(dims) == 3:
                a = a.rearrange("p (a b c) -> p a b c", a=dims[0], b=dims[1])
            return a

        def rounded(name, off, *dims):
            return nc.alloc_sbuf_tensor_at(name, [P, *dims], F32R, offset=base + 4 * off)[:]

        ident = cst[:, C_ID:C_ID + P]

        s_start, s_one, s_ct, s_sc = sems("s_start s_one s_ct s_sc")
        ada_w = [sem(f"ada_w{i}") for i in range(NW)]
        ada_high, ada_low, ada_mm, ada_row, ada_all = sems("ada_high ada_low ada_mm ada_row ada_all")
        ada_st = [sem(f"ada_st{i}") for i in range(NW)]
        par_in, par_tr, par_rdy = sems("par_in par_tr par_rdy")
        s_mod = sem("s_mod")
        xt_in, xt_st = ([sem(f"{s}{i}") for i in range(3)] for s in ("xt_in", "xt_st"))
        y_in, out_st = ([sem(f"{s}{i}") for i in range(2)] for s in ("y_in", "out_st"))
        y_mm, x_new, ss_rdy, rt_rdy, h_rdy, tr_rdy, ht_rdy, lg_rdy = sems(
            "y_mm x_new ss_rdy rt_rdy h_rdy tr_rdy ht_rdy lg_rdy")
        dv = sem("dv")
        wr_in, sc_rdy, mk_rdy, pos_rdy, sl_rdy, s_fill, s_scat = sems("wr_in sc_rdy mk_rdy pos_rdy sl_rdy s_fill s_scat")
        abw, abp = sems("abw0 abw1"), sems("abp0 abp1")
        wo_in = sems("wo_in0 wo_in1 wo_in2 wo_in3")
        rc_in, wp_in, ab_u, sg_rdy, glu_done, conv_s = sems("rc_in wp_in ab_u sg_rdy glu_done conv_s")
        pl_u, bp_rdy, pool_s, pg_mm, p_rdy, pad_z = sems("pl_u bp_rdy pool_s pg_mm p_rdy pad_z")
        ln_mu, ln_d, ln_sq, ln_sm, ln_ve, ln_sd, ln_n, ln_y = sems("ln_mu ln_d ln_sq ln_sm ln_ve ln_sd ln_n ln_y")
        moe = []
        for l in range(2):
            m = {s: sem(f"m{l}_{s}") for s in "used high low xg tx ab si g tg ye yst done".split()}
            m["w"] = [sem(f"m{l}_w{i}") for i in range(6)]
            moe.append(m)
        cw, hl_rdy, c_high, c_low, z_use = sems("cw hl_rdy c_high c_low z_use")
        xm_z, xm_mm, cv_s, xc_rdy, z_mm, z_rdy = sems("xm_z xm_mm cv_s xc_rdy z_mm z_rdy")
        z_st = sems("z_st0 z_st1")
        raw_in, bd_rdy, bt_mm, bt_ev, ge_mm, ge_rdy, g_mm, gr, ga, ar_st, stt_mm, st_rdy = sems(
            "raw_in bd_rdy bt_mm bt_ev ge_mm ge_rdy g_mm gr ga ar_st stt_mm st_rdy")
        v_mm, v_ev, kq_mm, k_ev, q_ev = sems("v_mm v_ev kq_mm k_ev q_ev")
        ab_in, hn_in = sems("ab_in hn_in")
        zl_in = sems("zl_in0 zl_in1")
        sS, dg, eE, aA, tT, aT, pV, lV, lX, hV, yT_mm, yT_ev = sems("sS dg eE aA tT aT pV lV lX hV yT_mm yT_ev")

        hT = at(0, KD, S)
        hall = at(0, NT, D)
        catT = at(6144, 2 * KD, S)
        ring = [at(18432 + 4096 * i, KD, 512) for i in range(2)]
        pring = [at(26624 + 4096 * i, KD, 512) for i in range(2)]
        wo = [at(26624, 2 * KD, 512), at(18432, 2 * KD, 512)]
        apad = [at(34816 + ROWS * RW * i, ROWS, RW) for i in range(2)]
        lpad = [at(37072 + 1536 * i, LROWS + 2 * PH, GRID_W) for i in range(2)]
        bpad = [at(40144 + 320 * i, CROWS, PW) for i in range(2)]
        ltmp = [at(o, LROWS + 2 * PH, GRID_W) for o in (40912, 6144 + 14 * S)]
        btmp = [at(o, CROWS, PW) for o in (40912, 6144 + 14 * S)]
        acc1 = at(42448, S)
        lnv = at(0, S)
        pooled = [at(43216 + S * i, S) for i in range(4)]
        rcnt = at(46288, 4, RC)
        wpool = at(47568, 8, 256)
        sg = [at(49616 + S * i, S) for i in range(2)]

        def chain_arrays(n):
            if n == 3:
                return dict(xt=[at(22528 + D * i, D) for i in range(2)],
                            mod=[None] * 3 + [at(24576 + D * i, D) for i in range(3)],
                            tmp=at(27648, D), htt=at(28672, KD, P))
            return dict(xt=[at(o, D) for o in (34928, 34928 + D, 12288)],
                        mod=[at(36976 + D * i, D) for i in range(6)],
                        tmp=at(43120, D), htt=at(44144, KD, P),
                        h=[at(6144 + D * i, D) for i in range(2)],
                        y=[[at(8192 + D * (2 * k + i), D) for i in range(2)] for k in range(2)])

        CH = [chain_arrays(n) for n in range(5)]
        MOD_OF = {0: ((0, 0), None), 1: ((0, 3), (0, 2)), 2: ((1, 0), (0, 5)), 3: ((1, 3), (1, 2)), 4: (None, (1, 5))}
        G_OF = {0: g_mix[0], 1: g_ffn[0], 2: g_mix[1], 3: g_ffn[1], 4: g_final}
        MODS = []
        for n in range(5):
            per = (2 if MOD_OF[n][0] else 0) + (1 if MOD_OF[n][1] else 0)
            MODS.append((MODS[-1] if MODS else 0) + 16 * (1 + per * (1 if n >= 3 else 2)))

        R0 = 45184
        r_sc, r_bi, r_m, r_t, r_w, r_f, r_sl, r_pos = (at(R0 + 96 * i, NT, NX) for i in range(8))
        r_big, r_big2 = at(R0 + 768, 480), at(R0 + 1248, 480)
        r_s = at(R0 + 1728, 400)

        wx = nc.alloc_sbuf_tensor_at("wx", [P, 6, 2, D], F32, offset=base + 4 * 6144)[:]
        wh = rounded("wh", 18432, NHL, D)
        wl = rounded("wl", 18432 + NHL * D, NHL, D)
        xg, gg, s0, yy = (at(D * i, D) for i in range(4))
        xTh, xTl = (rounded(f"xT{i}", 4 * D + D * i, KD, P) for i in range(2))
        gTh, gTl = (rounded(f"gT{i}", 45184 + D * i, KD, P) for i in range(2))

        adaw = nc.alloc_sbuf_tensor_at("adaw", [P, NW, KD, 512], F32, offset=base)[:]
        adah, adal = (rounded(f"ada_part{i}", 32768 + 8192 * i, 2, KD, 512) for i in range(2))
        scTh, scTl = (rounded(f"scT{i}", 49152 + D * i, KD, P) for i in range(2))
        bada = at(16384, 12 * D)
        stage = [at(28672 + 512 * i, 512) for i in range(NW)]
        csrc = at(30720, P)
        scT = at(30848, 2 * KD)
        psrc = at(30976, D)
        zt = at(12288, D)

        A_XM, A_XC = 6144, 6144 + KE * XM
        xm = at(A_XM, KE, XM)
        xc = at(A_XC, KE, XC)
        hTh, hTl = rounded("hTh", 0, KD, S), rounded("hTl", 44144, KD, S)
        craw = nc.alloc_sbuf_tensor_at("craw", [P, KD, 512], F32, offset=base + 4 * 30832)[:]
        cwh, cwl = rounded("cwh", 34928, KD, 512), rounded("cwl", 39024, KD, 512)
        BD = at(39024, 3, KE, P)
        geff = at(45168, 2 * KE, P)
        zst = [at(43120 + 512 * i, 512) for i in range(2)]
        raw = at(50288, 3, KE, 4)
        bdt = [at(30832 + 512 * i, 4, P) for i in range(2)]
        wg = at(31856, 3 * KE, NX)
        G, r_lf, r_b, r_a, r_M, r_x, r_zero = (at(32768 + S * i, S) for i in range(7))
        r_fl = at(30832, S)
        abc = at(0, 2 * H, S)
        qT = at(30832, KE, S_LAT)
        vv = [at(A_XM + HC * XM * h, NT, DH) for h in range(H)]
        Ef, Eb, A0, A1, AT = (at(45168 + S * i, S) for i in range(5))
        AA = [A0, A1]
        hv = at(49008, DH)
        zl = [at(49520 + DH * i, DH) for i in range(2)]
        hn = at(50544, DH)
        woc = [at(6144, KE, 512), at(14336, KE, 512)]

        w_ada_v = [w_ada[l].rearrange("(k p) n -> p k n", p=P) for l in range(2)]
        NA = 6 * D // 512

        def twice(i, s, n):
            return 2 * s + n if i is None else i * 2 + (2 * s + n)

        def ada_groups(eng):
            yield 0, 0, None
            with eng.Fori(1, NA // NW) as g:
                yield 0, g * NW, g * NW
            with eng.Fori(0, NA // NW) as g:
                yield 1, g * NW, g * NW + NA

        block = es.enter_context(nc.Block())

        def stores(n_to, j_to, s):
            return sum(1 for m, t, j in CHAINS if m in (1, 2, 3) and x_place(m, j) == s and (m < n_to or j <= j_to))

        def loads(n, j):
            return sum(1 for m, t, i in CHAINS if i <= j and x_place(m, i) == x_place(n, j))

        def await_stores(eng, n):
            for s in range(3):
                if stores(n, -1, s):
                    eng.wait_ge(xt_st[s], 16 * stores(n, -1, s))

        @block.sync
        def _(sp):
            sp.dma_start(cst[:], consts).then_inc(s_start, 16)
            sp.dma_start(csrc[0:KD, :], c.rearrange("a (k p) -> (a k) p", p=P)).then_inc(s_start, 16)
            sp.dma_start(csrc[KD:2 * KD, :], c_ctx.rearrange("(k p) -> k p", p=P)).then_inc(s_start, 16)
            sp.dma_start(wrt[:], w_router.rearrange("(k p) n -> p k n", p=P)).then_inc(wr_in, 16)
            sp.dma_start(brow[:], b_router.partition_broadcast(P)).then_inc(wr_in, 16)
            for v in range(2):
                sp.dma_start(bada[v:v + 1, :], b_ada.rearrange("l n -> (l n)").unsqueeze(0)).then_inc(s_start, 16)
            for l, n, i in ada_groups(sp):
                for s in range(NW):
                    if i is not None:
                        sp.wait_ge(ada_low, i * 2 + 2 * (s - NW + 1))
                    src = w_ada_v[l][:, :, n * 512 + s * 512:n * 512 + s * 512 + 512] if i is None else \
                        w_ada_v[l][:, :, bass.ds(n * 512 + s * 512, 512)]
                    sp.dma_start(adaw[:, s], src).then_inc(ada_w[s], 16)
                if i is None:
                    sp.dma_start(psrc[0:TAPS, :], w_dw_a[0]).then_inc(par_in, 16)
                    for r, v in enumerate((b_dw_a, ln_g_a, ln_b_a, b_pool.rearrange("a g d -> a (g d)"), pool_scale)):
                        sp.dma_start(psrc[TAPS + r:TAPS + r + 1, :], v).then_inc(par_in, 16)
                    for half in range(2):
                        r, cols = 64 + 5 * half, slice(half * D, half * D + D)
                        sp.dma_start(psrc[r:r + 4, :], w_conv_c[0][:, cols]).then_inc(par_in, 16)
                        sp.dma_start(psrc[r + 4:r + 5, :], b_conv_c[:, cols]).then_inc(par_in, 16)

            def load_mods(n):
                m = CH[n]["mod"]
                ss_, gate = MOD_OF[n]
                for v in range(1 if n >= 3 else 2):
                    o = 3 * (1 - v)
                    if ss_:
                        l, r = ss_
                        sp.dma_start(m[o], mods_d[l, v, (r + 1) * D:(r + 2) * D].partition_broadcast(P)).then_inc(s_mod, 16)
                        sp.dma_start(m[o + 1], mods_d[l, v, r * D:(r + 1) * D].partition_broadcast(P)).then_inc(s_mod, 16)
                    if gate:
                        l, r = gate
                        sp.dma_start(m[o + 2], mods_d[l, v, r * D:(r + 1) * D].partition_broadcast(P)).then_inc(s_mod, 16)
                sp.dma_start(CH[n]["tmp"], G_OF[n].partition_broadcast(P)).then_inc(s_mod, 16)

            def load_x(n, t, j):
                if n < 2:
                    src = ctx_in[0, t * P:(t + 1) * P, :] if t < CT else x[0, (t - CT) * P:(t - CT + 1) * P, :]
                else:
                    src = xs_d[n - 1][t * P:(t + 1) * P, :]
                s = x_place(n, j)
                sp.dma_start(CH[n]["xt"][s], src).then_inc(xt_in[s], 16)

            wc = w_in_c[0].rearrange("(k p) n -> p k n", p=P)

            def chain_start(n):
                await_stores(sp, n)
                for t, j in tiles_of(n)[:2]:
                    load_x(n, t, j)
                load_mods(n)

            def chain(n):
                tiles = tiles_of(n)
                ahead = 3 if n in (2, 4) else 2
                if ahead == 3:
                    load_x(n, *tiles[2])
                for i, (t, j) in enumerate(tiles):
                    s = x_place(n, j)
                    if n in (1, 2, 3):
                        sp.wait_ge(x_new, j + 1 - NT)
                        sp.dma_start(xs_d[n][t * P:(t + 1) * P, :], CH[n]["xt"][s]).then_inc(xt_st[s], 16)
                    if n == 4:
                        sp.wait_ge(h_rdy, j + 1)
                        sp.dma_start(out[0, (t - CT) * P:(t - CT + 1) * P, :], CH[4]["h"][j % 2]).then_inc(out_st[j % 2], 16)
                    if n == 2 and i == 0:
                        sp.dma_start(craw, wc[:, :, 0:512]).then_inc(cw, 16)
                    if i + ahead < len(tiles):
                        sp.wait_ge(h_rdy, j + 1)
                        if n in (1, 2, 3):
                            sp.wait_ge(xt_st[s], 16 * stores(0, j, s))
                        load_x(n, *tiles[i + ahead])

            def expert_weights(l, e, b, groups, ahead=0):
                m = moe[l]
                for g in groups:
                    kk, mat = (g // 2, (w1, w3)[g % 2]) if g < 8 else (g - 8, w2)
                    if g >= 6:
                        sp.wait_ge(m["low"], made(b, "chunk", 2 * g - 11))
                    elif b is not None:
                        sp.wait_ge(m["low"], made(b, "chunk", 2 * g + 13, PARTS * (ahead - 1)))
                    src = mat[l].rearrange("e (k p) n -> p (e k) n", p=P)[:, bass.ds(e * KD + 2 * kk, 2), :]
                    sp.dma_start(wx[:, g % 6], src).then_inc(m["w"][g % 6], 16)

            def experts(l):
                expert_weights(l, 0, None, range(6, 12))
                sp.wait_ge(sl_rdy, l + 1)
                nb = sp.value_load(table[0:1, 31:32], min_val=NX, max_val=NB - 1)
                expert_weights(l, 1, 0, range(2), 1)
                with sp.Fori(1, nb) as b:
                    e = sp.value_load(table[0:1, bass.ds(b, 1)], min_val=0, max_val=NX - 1)
                    after = sp.value_load(table[0:1, bass.ds(b + 1, 1)], min_val=0, max_val=NX - 1)
                    expert_weights(l, e, b, range(2, 12))
                    expert_weights(l, after, b, range(2), 1)

            sp.wait_ge(ada_all, 1)
            chain_start(0)
            wi = w_in_ab[0].rearrange("(k p) n -> p k n", p=P)
            woa = w_out_ab[0].rearrange("(k p) n -> p k n", p=P)

            def panel(g):
                for q in range(2):
                    sp.dma_start(ring[g % 2][:, :, 256 * q:256 * q + 256],
                                 wi[:, :, q * D + g * 256:q * D + (g + 1) * 256]).then_inc(abw[g % 2], 16)

            chain(0)
            panel(0)
            panel(1)
            for g in range(2):
                sp.dma_start(pring[g], wi[:, :, 2 * D + g * 512:2 * D + (g + 1) * 512]).then_inc(abp[g], 16)
            sp.dma_start(rcnt, rcounts.rearrange("a (w s) -> (a w) s", w=4).partition_broadcast(P)).then_inc(rc_in, 16)
            sp.dma_start(wpool, w_pool[0].rearrange("g (k p) n -> p (g k) n", p=P)).then_inc(wp_in, 16)
            for g in range(2, 4):
                sp.wait_ge(ab_u, 2 * (g - 1))
                panel(g)
            for half in range(2):
                sp.wait_ge(pl_u, KD) if half == 0 else sp.wait_ge(ab_u, KD)
                for q in range(2):
                    sp.dma_start(wo[half][:, 8 * q:8 * q + 8, :], woa[:, 8 * q:8 * q + 8, 512 * half:512 * half + 512]
                                 ).then_inc(wo_in[2 * half + q], 16)
            sp.wait_ge(conv_s, CONV_OPS * KD)
            sp.wait_ge(p_rdy, KD)
            chain_start(1)
            chain(1)
            sp.wait_ge(y_mm, NT)
            expert_weights(0, 0, None, range(6))
            sp.wait_ge(h_rdy, 2 * NT)
            chain_start(2)
            experts(0)
            sp.wait_ge(moe[0]["done"], 1)
            chain(2)
            for i, (wm) in enumerate((w_q, w_k, w_v)):
                sp.dma_start(raw[:, i], wm[0].rearrange("(t n) i o -> (n i) t o", n=32)).then_inc(raw_in, 16)
            for i in range(4):
                sp.dma_start(gbias[32 * i:32 * i + H, :],
                             b_gates[0, GATE_COL[i] * H:(GATE_COL[i] + 1) * H].unsqueeze(1)).then_inc(raw_in, 16)
            for g in range(1, 8):
                sp.wait_ge(c_low, 4 * g if g <= 4 else KE + KD * (g - 4))
                sp.dma_start(craw, wc[:, :, g * 512:(g + 1) * 512]).then_inc(cw, 16)
            sp.wait_ge(z_mm, 16)
            sp.dma_start(wg, w_gates[0].rearrange("(k p) n -> p k n", p=P)).then_inc(wp_in, 16)
            sp.wait_ge(gr, R_A)
            for d in range(2):
                sp.dma_start(arow_d[4 * d:4 * d + 4, :], r_a[32 * d:32 * d + 4, :]).then_inc(ar_st, 16)
            sp.wait_ge(ar_st, 32)
            sp.dma_start(abc.rearrange("p a b -> p (a b)"),
                         arow_d.rearrange("a b -> (a b)").partition_broadcast(P)).then_inc(ab_in, 16)
            for s in range(2):
                sp.wait_ge(z_st[s], 16 * 8)
            for u in range(16):
                h, i = u // 4, u % 4
                if u == 0:
                    sp.wait_ge(g_mm, 1)
                if u >= 2:
                    sp.wait_ge(hV, u - 1)
                sp.dma_start(zl[u % 2], zs_d[i * P:(i + 1) * P, h * DH:(h + 1) * DH]).then_inc(zl_in[u % 2], 16)
                if i == 0:
                    if h:
                        sp.wait_ge(hV, u)
                    sp.dma_start(hn, hn_g[0, h * DH:(h + 1) * DH].partition_broadcast(P)).then_inc(hn_in, 16)
                if u == 13:
                    sp.wait_ge(pV, 12)
                    wov = w_out_c[0].rearrange("(k p) n -> p k n", p=P)
                    for q in range(2):
                        sp.dma_start(woc[0][:, 8 * q:8 * q + 8, :], wov[:, 8 * q:8 * q + 8, 0:512]).then_inc(wo_in[q], 16)
            sp.wait_ge(pV, 16)
            for q in range(2):
                sp.dma_start(woc[1][:, 8 * q:8 * q + 8, :], wov[:, 8 * q:8 * q + 8, 512:1024]).then_inc(wo_in[2 + q], 16)
            chain_start(3)
            chain(3)
            sp.wait_ge(y_mm, NT + 4)
            expert_weights(1, 0, None, range(6))
            chain_start(4)
            experts(1)
            sp.wait_ge(moe[1]["done"], 1)
            chain(4)
            for s in range(2):
                sp.wait_ge(out_st[s], 32)

        @block.gpsimd
        def _(pool):
            pool.wait_ge(s_one, 1)
            pool.dma_start(arow_d[0:1, 0:16], ones[0:1, 0:16]).then_inc(ada_st[NW - 1], 16)
            for l, n, i in ada_groups(pool):
                for s in range(NW):
                    pool.wait_ge(ada_row, s + 1 if i is None else i + s + 1)
                    dst = mods_d[l, :, n * 512 + s * 512:n * 512 + s * 512 + 512] if i is None else \
                        mods_d[l, :, bass.ds(n * 512 + s * 512, 512)]
                    pool.dma_start(dst, stage[s][0:2, :]).then_inc(ada_st[s], 16)
            pool.wait_ge(h_rdy, NT)
            for i in range(2):
                pool.memset(apad[i], 0.0).then_inc(pad_z, 1)
                pool.memset(bpad[i], 0.0).then_inc(pad_z, 1)
                pool.memset(lpad[i], 0.0).then_inc(pad_z, 1)
            pool.memset(zt, 0.0).then_inc(pad_z, 1)
            pool.wait_ge(pad_z, 7)
            pool.dma_start(buf_v[:, :, :], bc(zt, 1, NB)).then_inc(s_fill, 16)
            pool.wait_ge(rc_in, 16)
            n = 0

            def step(ins):
                nonlocal n
                n += 1
                ins.then_inc(pool_s, 1)
                pool.wait_ge(pool_s, n)

            for p in range(KD):
                g = p // 2
                b = bpad[p % 2]
                if p == 1:
                    pool.wait_ge(s_fill, 16)
                pool.wait_ge(bp_rdy, p + 1)
                if p >= 4 and p % 2 == 0:
                    pool.wait_ge(pg_mm, p - 2)
                step(pool.tensor_copy(b[:, 0:CROWS - 1, PH + GRID_W:PW], b[:, 1:CROWS, PH:2 * PH]))
                step(pool.tensor_copy(b[:, 1:CROWS, 0:PH], b[:, 0:CROWS - 1, GRID_W:GRID_W + PH]))
                win = WINDOWS[g]
                dst = pooled[p % 4].rearrange("p (r w) -> p r w", w=GRID_W)
                cur, first = lpad[p % 2], PH - win // 2
                for lv in range(g + 1):
                    nxt, w_ = ltmp[lv % 2], 1 << lv
                    rows = LROWS + win - 2 * w_
                    step(pool.tensor_tensor(nxt[:, 0:rows], cur[:, first:first + rows],
                                            cur[:, first + w_:first + w_ + rows], ALU.add))
                    cur, first = nxt, 0
                step(pool.tensor_tensor(dst[:, CROWS:], cur[:, 0:LROWS], bc(rcnt[:, g, S_CTX:], 2, GRID_W), ALU.mult))
                step(pool.tensor_tensor(dst[:, CROWS:], dst[:, CROWS:], lpad[p % 2][:, PH:PH + LROWS], ALU.subtract))
                cur, first, wdt = b, PH - win // 2, GRID_W + win
                for lv in range(g + 1):
                    nxt, w_ = btmp[lv % 2], 1 << lv
                    wdt = GRID_W + win - 2 * w_
                    step(pool.tensor_tensor(nxt[:, :, 0:wdt], cur[:, :, first:first + wdt],
                                            cur[:, :, first + w_:first + w_ + wdt], ALU.add))
                    cur, first = nxt, 0
                step(pool.tensor_tensor(dst[:, 0:CROWS], cur[:, :, 0:GRID_W],
                                        rcnt[:, g, 0:S_CTX].rearrange("p (r w) -> p r w", w=GRID_W), ALU.mult))
                step(pool.tensor_tensor(dst[:, 0:CROWS], dst[:, 0:CROWS], b[:, :, PH:PH + GRID_W], ALU.subtract))
                assert n == POOL_DONE[p]

            def scatter(l):
                pool.wait_ge(sl_rdy, l + 1)
                tl = tiles_of(1 + 2 * l)
                for k in range(2):
                    for t, j in tl:
                        pool.indirect_dma_start(buf_d, bass.IndirectOffsetOnAxis(ap=slots[:, k, t:t + 1], axis=0),
                                                hall[:, t, :], None).then_inc(s_scat, 16)

            def experts(l):
                m = moe[l]
                pool.wait_ge(s_scat, 16 * 2 * (NT if l == 0 else NT + 4))
                pool.dma_start(xg, buf_v[:, 0, :]).then_inc(m["xg"], 16)
                pool.wait_ge(m["ye"], 1)
                pool.dma_start(buf_v[:, NB - 1, 0:16], yy[:, 0:16]).then_inc(m["yst"], 16)
                nb = pool.value_load(table[0:1, 31:32], min_val=NX, max_val=NB - 1)
                with pool.Fori(0, nb) as b:
                    pool.wait_ge(m["tx"], b + 1)
                    pool.dma_start(xg, buf_v[:, bass.ds(b + 1, 1), :].rearrange("p a d -> p (a d)")).then_inc(m["xg"], 16)
                    pool.wait_ge(m["ye"], b + 2)
                    pool.dma_start(buf_v[:, bass.ds(b, 1), :].rearrange("p a d -> p (a d)"), yy).then_inc(m["yst"], 16)

            def gather(n):
                pool.wait_ge(moe[n // 2 - 1]["done"], 1)
                for t, j in tiles_of(n):
                    s = j % 2
                    if j - 2 >= tiles_of(n)[0][1]:
                        pool.wait_ge(x_new, j - 1 - NT)
                    for k in range(2):
                        pool.indirect_dma_start(CH[n]["y"][k][s], None, buf_d,
                                                bass.IndirectOffsetOnAxis(ap=slots[:, k, t:t + 1], axis=0)
                                                ).then_inc(y_in[s], 16)

            scatter(0)
            experts(0)
            gather(2)
            pool.wait_ge(tr_rdy, 3 * NT)
            await_stores(pool, 3)
            pool.memset(xm[:, :, 0:2], 0.0).then_inc(xm_z, 1)
            pool.memset(xm[:, :, 2 + S_CTX:4 + S_CTX], 0.0).then_inc(xm_z, 1)
            pool.memset(xm[:, :, XM - 1:XM], 0.0).then_inc(xm_z, 1)
            pool.wait_ge(raw_in, 48 + 64)
            pool.wait_ge(z_mm, 16)

            def diagonal(i, t):
                return pool.tensor_tensor(BD[:, i, t].rearrange("p (g o) -> p g o", o=4),
                                          bc(cst[:, C_G4:C_G4 + 32], 2, 4), bc(raw[:, i, t], 1, 32), ALU.mult)

            for t in range(KE):
                diagonal(0, t)
                diagonal(1, t).then_inc(bd_rdy, 1)
            for s in range(2):
                pool.wait_ge(z_st[s], 16 * 8)
            for t in range(KE):
                diagonal(2, t).then_inc(bd_rdy, 1)
            pool.wait_ge(ab_in, 16)
            for u in range(16):
                h, i = u // 4, u % 4
                o = S_CTX + P * i
                if u == 0:
                    pool.wait_ge(g_mm, 1)
                else:
                    pool.wait_ge(aA, 4 * u)
                pool.tensor_tensor(Ef[:, o:o + P], abc[:, h, o:o + P], cst[:, C_NF:C_NF + P], ALU.add).then_inc(dg, 1)
                pool.tensor_tensor(Eb[:, o:o + P], abc[:, H + h, o:o + P], cst[:, C_NB_:C_NB_ + P], ALU.add).then_inc(dg, 1)
            scatter(1)
            experts(1)
            gather(4)

        @block.tensor
        def _(pe):
            def mm(bank_ap, lhsT, rhs, first, last):
                return pe.matmul(bank_ap, lhsT, rhs, start=first, stop=last)

            pe.wait_ge(s_start, 16 * 5)
            pe.transpose(ps[:, 7, 0:2 * KD], csrc[0:2 * KD, :], ident[0:2 * KD, 0:2 * KD]).then_inc(s_ct, 1)
            pe.wait_ge(s_sc, 3)

            def three(out_, ah, al, bh, bl, first, last):
                mm(out_, ah, bh, first, False)
                mm(out_, ah, bl, False, False)
                return mm(out_, al, bh, False, last)

            for l, n, i in ada_groups(pe):
                for s in range(NW):
                    if i is not None:
                        pe.wait_ge(ada_row, i + s - NW + 1)
                    for k in range(KD):
                        if k % HK == 0:
                            pe.wait_ge(ada_low, twice(i, s, k // HK + 1))
                        ins = three(ps[:, s, :], scTh[:, k, :], scTl[:, k, :], adah[:, s % 2, k, :], adal[:, s % 2, k, :],
                                    k == 0, k == KD - 1)
                        if k % HK == HK - 1:
                            ins.then_inc(ada_mm, 1)
                if i is None:
                    pe.wait_ge(par_in, 16 * 10)
                    for k in range(KD):
                        pe.transpose(ps[:, 5, k * NPAR:(k + 1) * NPAR], psrc[0:NPAR, k * P:(k + 1) * P],
                                     ident[0:NPAR, 0:NPAR])
                    for k in range(KD):
                        ins = pe.transpose(ps[:, 6, 10 * k:10 * k + 10], psrc[64:74, k * P:(k + 1) * P],
                                           ident[64:74, 64:74])
                    ins.then_inc(par_tr, 1)

            def to_channels(n, t, j):
                src = hall[:, t, :] if n in (1, 3) else CH[n]["h"][j % 2]
                pe.wait_ge(h_rdy, j + 1)
                if j:
                    pe.wait_ge(ht_rdy, j)
                if n == 2 and t:
                    pe.wait_ge(hl_rdy, t)
                for k in range(KD):
                    ins = pe.transpose(ps[:, 4 + k // 4, (k % 4) * P:(k % 4 + 1) * P], src[:, k * P:(k + 1) * P], ident)
                ins.then_inc(tr_rdy, 1)

            def route(n, t, j):
                pe.wait_ge(ht_rdy, j + 1)
                for k in range(KD):
                    ins = mm(ps[:, 6, t * NX:(t + 1) * NX], CH[n]["htt"][:, k, :], wrt[:, k, :], k == 0, k == KD - 1)
                ins.then_inc(lg_rdy, 1)

            def project(n, t, j, acts, w, kn):
                b0 = 2 * (j % 2)
                if j - 2 >= tiles_of(n)[0][1]:
                    pe.wait_ge(x_new, j - 1 - NT)
                order = [*range(KD, kn), *range(KD)] if n == 1 else range(kn)
                for i, k in enumerate(order):
                    if n == 1 and t == 0 and k < KD:
                        pe.wait_ge(ln_y, k + 1)
                    for q in range(2):
                        ins = mm(ps[:, b0 + q, :], acts(k, t), w[q][:, k, :], i == 0, i == kn - 1)
                ins.then_inc(y_mm, 1)

            def projected_chain(n, acts, w, kn):
                tl = tiles_of(n)
                for i in range(len(tl) + 2):
                    if i < len(tl):
                        project(n, *tl[i], acts, w, kn)
                    if i >= 2:
                        route(n, *tl[i - 2])
                    if 1 <= i <= len(tl):
                        to_channels(n, *tl[i - 1])

            def positions(l):
                pe.wait_ge(mk_rdy, l + 1)
                t0 = tiles_of(1 + 2 * l)[0][0]

                def sums(lhsT, lo, hi, shift, first, last):
                    return mm(ps[:, 7, (lo + shift) * NX:hi * NX], lhsT,
                              r_m[:, lo:hi - shift, :].rearrange("p t e -> p (t e)"), first, last)

                before = cst[:, C_TRI:C_TRI + P]
                sums(before, t0, t0 + 1, 0, True, True)
                sums(before, t0 + 1, NT, 0, True, False)
                for d in range(NT - t0 - 1, 0, -1):
                    sums(ones[:], t0, NT, d, False, d == 1)
                mm(ps[:, 7, P:P + (NT - t0) * NX], ones[:], r_m[:, t0:, :].rearrange("p t e -> p (t e)"), True, True
                   ).then_inc(pos_rdy, 1)

            def turn_x():
                for k in range(KD):
                    ins = pe.transpose(ps[:, 4 + k // 4, (k % 4) * P:(k % 4 + 1) * P], xg[:, k * P:(k + 1) * P], ident)
                return ins

            def parts(bank, ah, al, slot, q, first, last):
                cols = slice(512 * q, 512 * q + 512)
                return three(bank, ah, al, wh[:, slot, cols], wl[:, slot, cols], first, last)

            def experts(l):
                m = moe[l]
                pe.sem_inc(m["used"], 8)
                pe.wait_ge(m["xg"], 16)
                turn_x().then_inc(m["tx"], 1)
                nb = pe.value_load(table[0:1, 31:32], min_val=NX, max_val=NB - 1)
                with pe.Fori(0, nb) as b:
                    for kk in range(KD // 2):
                        pe.wait_ge(m["low"], made(b, "chunk", 4 * kk + 3))
                        for q in range(2):
                            for i in range(2):
                                k = 2 * kk + i
                                for mat in range(2):
                                    ins = parts(ps[:, 2 * q + mat, :], xTh[:, k, :], xTl[:, k, :],
                                                (4 * kk + 2 * mat + i) % NHL, q, k == 0, k == KD - 1)
                            if kk == KD // 2 - 1 and q == 0:
                                ins.then_inc(m["ab"], 1)
                        ins.then_inc(m["used"], 1)
                    pe.wait_ge(m["xg"], b * 16 + 32)
                    turn_x().then_inc(m["tx"], 1)
                    for q in range(2):
                        pe.wait_ge(m["g"], b * 2 + (q + 1))
                        for k in range(4):
                            ins = pe.transpose(ps[:, q, k * P:(k + 1) * P], gg[:, (4 * q + k) * P:(4 * q + k + 1) * P], ident)
                        ins.then_inc(m["tg"], 1)
                    pe.wait_ge(m["ye"], b + 1)
                    for kk in range(KD // 2):
                        if kk % 2 == 0:
                            pe.wait_ge(m["low"], made(b, "g", kk // 2))
                        if kk > 1:
                            pe.wait_ge(m["low"], made(b, "chunk", 2 * kk + 17))
                        for i in range(2):
                            k = 2 * kk + i
                            for q in range(2):
                                ins = parts(ps[:, 6 + q, :], gTh[:, k, :], gTl[:, k, :], k % NHL, q, k == 0, k == KD - 1)
                        ins.then_inc(m["used"], 1)

            pe.wait_ge(par_rdy, 1)
            for t, j in tiles_of(0):
                to_channels(0, t, j)
            pe.wait_ge(ht_rdy, NT)

            def wide(start, lhs, rhs, kn):
                cut = 512 if start % 512 == 0 else 256
                for k in range(kn):
                    mm(psf[:, start:start + cut], lhs(k), rhs(k)[:, 0:cut], k == 0, k == kn - 1)
                    ins = mm(psf[:, start + cut:start + S], lhs(k), rhs(k)[:, cut:S], k == 0, k == kn - 1)
                return ins

            for kind, i, before in AB_ORDER:
                if kind in ("value", "gate"):
                    q, g, o = int(kind == "gate"), i // 2, (i % 2) * P
                    if q == 0 and i % 2 == 0:
                        pe.wait_ge(abw[g % 2], 32 * (g // 2 + 1))
                    if q == 0 and i >= 2:
                        pe.wait_ge(glu_done, i - 1)
                    ins = wide(1536 * (i % 2) + S * q, lambda k: ring[g % 2][:, k, 256 * q + o:256 * q + o + P],
                               lambda k: hT[:, k, :], KD)
                    if q:
                        ins.then_inc(ab_u, 1)
                    continue
                if before:
                    pe.wait_ge(bp_rdy if before[0] == "pool" else p_rdy, before[1] + 1)
                if kind == "pool":
                    g, o = i // 4, (i % 4) * P
                    if i % 4 == 0:
                        pe.wait_ge(abp[g], 16)
                    wide(3072, lambda k: pring[g][:, k, o:o + P], lambda k: hT[:, k, :], KD).then_inc(pl_u, 1)
                else:
                    g, q = i // 2, i % 2
                    if i == 0:
                        pe.wait_ge(wp_in, 16)
                    pe.wait_ge(pool_s, POOL_DONE[2 * g + 1])
                    wide(3072, lambda k: wpool[:, 2 * g + k, q * P:(q + 1) * P],
                         lambda k: pooled[(2 * g + k) % 4], 2).then_inc(pg_mm, 1)
            pe.wait_ge(glu_done, KD)
            for ct in range(KD):
                pe.wait_ge(conv_s, CONV_OPS * (ct + 1))
                for q, n in ((0, 512), (1, S - 512)):
                    ins = mm(ps[:, q, 0:n], onesd[:], catT[:, ct, 512 * q:512 * q + n], ct == 0, ct == KD - 1)
            ins.then_inc(ln_mu, 1)
            for ct in range(KD):
                pe.wait_ge(ln_sq, ct + 1)
                for q, n in ((0, 512), (1, S - 512)):
                    ins = mm(ps[:, 2 + q, 0:n], onesd[:], sg[ct % 2][:, 512 * q:512 * q + n], ct == 0, ct == KD - 1)
                ins.then_inc(ln_sm, 1)
            pe.wait_ge(ln_ve, 1)
            pe.wait_ge(p_rdy, KD)
            for q in range(4):
                pe.wait_ge(wo_in[q], 16)
            pe.wait_ge(wr_in, 32)
            projected_chain(1, lambda k, t: catT[:, k, t * P:(t + 1) * P], wo, 2 * KD)
            positions(0)
            experts(0)
            for t, j in tiles_of(2):
                to_channels(2, t, j)
            for ct in range(KE):
                cols = slice(ct % 4 * P, ct % 4 * P + P)
                pe.wait_ge(c_low, ct + 1)
                if ct >= 4:
                    pe.wait_ge(cv_s, CV_OPS * (ct - 4) + 2)
                b = 2 * (ct % 4)
                for k in range(KD):
                    for o, toks in ((ps[:, b, :], slice(0, 512)), (ps[:, b + 1, 0:S - 512], slice(512, S))):
                        ins = three(o, cwh[:, k, cols], cwl[:, k, cols], hTh[:, k, toks], hTl[:, k, toks],
                                    k == 0, k == KD - 1)
                ins.then_inc(xm_mm, 1)
            for z in range(16):
                g, i = z // 4, z % 4
                toks = slice(S_CTX + i * P, S_CTX + (i + 1) * P)
                if z < 8:
                    pe.wait_ge(cv_s, CV_OPS * (12 + z // 2) + 2)
                else:
                    pe.wait_ge(z_rdy, z - 7)
                for k in range(KD):
                    if i == 0:
                        pe.wait_ge(c_low, KE + KD * g + k + 1)
                    ins = three(ps[:, z % 8, :], hTh[:, k, toks], hTl[:, k, toks], cwh[:, k, :], cwl[:, k, :],
                                k == 0, k == KD - 1)
                    if i == 3 and k < KD - 1:
                        ins.then_inc(z_use, 1)
                ins.then_inc(z_mm, 1)
            pe.wait_ge(z_rdy, 16)
            pe.wait_ge(wp_in, 32)

            def turn_bd(bt):
                pe.wait_ge(bd_rdy, 2 * bt + 2 if bt < 8 else KE + 4 * (bt - 7))
                if bt >= 2:
                    pe.wait_ge(bt_ev, bt - 1)
                for i, (m_, t) in enumerate(BATCH[bt]):
                    ins = pe.transpose(ps[:, bt % 2, i * P:(i + 1) * P], BD[:, m_, t, :], ident)
                ins.then_inc(bt_mm, 1)

            turn_bd(0)
            for bt in range(12):
                if bt + 1 < 12:
                    turn_bd(bt + 1)
                pe.wait_ge(bt_ev, bt + 1)
                for i, (m_, t) in sorted(enumerate(BATCH[bt]), key=lambda e: (e[1][1], e[1][0])):
                    row = (t if m_ < 2 else KE + t) * NX
                    ins = mm(ps[:, 2, row:row + NX], bdt[bt % 2][:, i, :], wg[:, m_ * KE + t, :], m_ != 1, m_ != 0)
                if bt == 11:
                    ins.then_inc(ge_mm, 1)
                else:
                    ins.then_inc(ge_mm, 1)
            pe.wait_ge(ge_rdy, 4)
            for t in range(KE):
                pe.wait_ge(xc_rdy, t + 1)
                mm(ps[:, 4, 256:512], geff[:, t, :], xc[:, t, 0:S_CTX], t == 0, False)
                mm(ps[:, 5, :], geff[:, t, :], xc[:, t, S_CTX + 2:], t == 0, False)
            for t in range(KE):
                mm(ps[:, 4, 256:512], geff[:, KE + t, :], xm[:, t, 2:2 + S_CTX], False, t == KE - 1)
                ins = mm(ps[:, 5, :], geff[:, KE + t, :], xm[:, t, 4 + S_CTX:4 + S], False, t == KE - 1)
            ins.then_inc(g_mm, 1)
            for h in range(H):
                pe.wait_ge(gr, R_G) if h == 0 else pe.wait_ge(v_ev, 6 * h)
                for tt in range(NT):
                    o = 2 + tt * P if tt < CT else 4 + tt * P
                    for cc in range(HC):
                        t = h * HC + cc
                        ins = mm(ps[:, tt, cc * P:(cc + 1) * P], xm[:, t, o:o + P], BD[:, 2, t, :], True, True)
                ins.then_inc(v_mm, 1)
            pe.wait_ge(gr, R_M)
            pe.wait_ge(ga, A_FL)
            for i in range(4):
                o = S_CTX + i * P
                pe.transpose(ps[:, 6, 64 * i:64 * i + 64], r_M[0:64, o:o + P], ident[0:64, 0:64])
                ins = pe.transpose(ps[:, 7, 64 * i:64 * i + 64], r_fl[0:64, o:o + P], ident[0:64, 0:64])
            ins.then_inc(stt_mm, 1)
            pe.wait_ge(v_ev, 6 * H)
            pe.wait_ge(st_rdy, 2)
            for t in range(KE):
                b0 = 4 * (t % 2)
                if t >= 2:
                    pe.wait_ge(k_ev, 2 * (t - 1))
                    pe.wait_ge(q_ev, t - 1)
                mm(ps[:, b0, 256:512], BD[:, 1, t, :], xc[:, t, 0:S_CTX], True, True)
                mm(ps[:, b0 + 1, :], BD[:, 1, t, :], xc[:, t, S_CTX + 2:], True, True)
                mm(ps[:, b0 + 2, :], BD[:, 0, t, :], xc[:, t, S_CTX + 2:], True, True).then_inc(kq_mm, 1)
            pe.wait_ge(k_ev, 2 * KE)
            pe.wait_ge(q_ev, KE)

            def scores(u):
                h, i = u // 4, u % 4
                b0 = 2 * (u % 2)
                if u >= 2:
                    pe.wait_ge(aA, 4 * (u - 2) + 1)
                for cc in range(HC):
                    t = h * HC + cc
                    lhs = qT[:, t, i * P:(i + 1) * P]
                    mm(ps[:, b0, 256:512], lhs, xc[:, t, 0:S_CTX], cc == 0, cc == HC - 1)
                    ins = mm(ps[:, b0 + 1, :], lhs, xc[:, t, S_CTX + 2:], cc == 0, cc == HC - 1)
                ins.then_inc(sS, 1)

            def turn_y(u):
                pe.wait_ge(hV, u + 1)
                if u:
                    pe.wait_ge(yT_ev, u)
                for cc in range(HC):
                    ins = pe.transpose(ps[:, 7, cc * P:(cc + 1) * P], hv[:, cc * P:(cc + 1) * P], ident)
                ins.then_inc(yT_mm, 1)

            scores(0)
            for u in range(16):
                h, i = u // 4, u % 4
                if u + 1 < 16:
                    scores(u + 1)
                pe.wait_ge(aA, 4 * u + 4)
                if u:
                    pe.wait_ge(aT, u)
                for s in range(NT):
                    ins = pe.transpose(ps[:, 4 + s // 4, (s % 4) * P:(s % 4 + 1) * P], AA[u % 2][:, s * P:(s + 1) * P], ident)
                ins.then_inc(tT, 1)
                if u:
                    turn_y(u - 1)
                pe.wait_ge(aT, u + 1)
                for s in range(NT):
                    ins = mm(ps[:, 6, :], AT[:, s * P:(s + 1) * P], vv[h][:, s, :], s == 0, s == NT - 1)
                ins.then_inc(pV, 1)
            turn_y(15)
            pe.wait_ge(yT_ev, 16)
            for q in range(4):
                pe.wait_ge(wo_in[q], 32)
            projected_chain(3, lambda k, t: qT[:, k, (t - CT) * P:(t - CT + 1) * P], woc, KE)
            positions(1)
            experts(1)

        @block.scalar
        def _(act):
            def go(out_, in_, f, **kw):
                return act.activation(out_, in_, f, **kw)

            act.wait_ge(s_ct, 1)
            go(scT, ps[:, 7, 0:2 * KD], ACT.Silu).then_inc(s_sc, 1)
            act.wait_ge(s_sc, 1)
            act.wait_ge(s_one, 5)
            scv = scT.rearrange("p (v k) -> p k v", v=2)
            go(scTh[:, :, 0:2], scv, ACT.Copy).then_inc(s_sc, 1)
            for l, n, i in ada_groups(act):
                for s in range(NW):
                    act.wait_ge(ada_w[s], 16 if i is None else 4 * i + 16)
                    for q in range(2):
                        if i is not None or s >= 2:
                            act.wait_ge(ada_mm, twice(i, s, q - 3))
                        rows = slice(HK * q, HK * q + HK)
                        go(adah[:, s % 2, rows], adaw[:, s, rows], ACT.Copy).then_inc(ada_high, 1)
            for s in range(NW):
                act.wait_ge(ada_st[s], 16 * (2 * NA // NW + (s == NW - 1)))
            go(ss[:, 0:1], ones[:, 0:1], ACT.Copy).then_inc(ada_all, 1)

            def norm(n, t, j):
                s = j % 2
                dst = hall[:, t, :] if n in (1, 3) else CH[n]["h"][s]
                if n in (0,):
                    act.wait_ge(xt_in[x_place(n, j)], 16 * loads(n, j))
                else:
                    act.wait_ge(x_new, j + 1 - NT)
                if n in (0, 2) and j - 2 >= tiles_of(n)[0][1]:
                    act.wait_ge(tr_rdy, j - 1)
                if n == 4 and j - 2 >= tiles_of(n)[0][1]:
                    act.wait_ge(out_st[s], 16 * ((j - tiles_of(4)[0][1]) // 2))
                if j >= 2:
                    act.wait_ge(h_rdy, j - 1)
                go(dst, CH[n]["xt"][x_place(n, j)], ACT.Square, accum_out=ss[:, s:s + 1]).then_inc(ss_rdy, 1)
                act.wait_ge(ss_rdy, j + 1)
                go(rt[:, s:s + 1], ss[:, s:s + 1], ACT.Sqrt, scale=1.0 / D, bias=epsc[:]).then_inc(rt_rdy, 1)

            def turned(n, t, j):
                act.wait_ge(tr_rdy, j + 1)
                if n in (1, 3):
                    if t > tiles_of(n)[0][0]:
                        act.wait_ge(lg_rdy, lg_before(n, t))
                    dst = CH[n]["htt"]
                else:
                    dst = (hTh if n == 2 else hT)[:, :, t * P:(t + 1) * P]
                go(dst, psf[:, 4 * 512:6 * 512].rearrange("p (k n) -> p k n", n=P), ACT.Copy).then_inc(ht_rdy, 1)

            def chain(n):
                tl = tiles_of(n)
                for i in range(len(tl) + 1):
                    if i < len(tl):
                        norm(n, *tl[i])
                    if i and n < 4:
                        turned(n, *tl[i - 1])
                if n in (1, 3):
                    l = n // 2
                    act.wait_ge(lg_rdy, lg_before(n, NT))
                    t0 = tl[0][0]
                    go(r_sc[:, t0:, :].rearrange("p t e -> p (t e)"), ps[:, 6, t0 * NX:NT * NX], ACT.Sigmoid).then_inc(sc_rdy, 1)

            def experts(l):
                m = moe[l]

                def high(b, r, ahead=0):
                    g = r // 2
                    if r % 2 == 0:
                        act.wait_ge(m["w"][g % 6], b * 32 + (ahead * 32 + 16 * (g // 6 + 1)))
                    if r >= 8:
                        act.wait_ge(m["used"], b * 8 + (8 + (r - 8) // 4 + 1))
                    else:
                        act.wait_ge(m["used"], b * 8 + (8 * ahead + 4 + r // 2 + 1))
                    go(wh[:, r % NHL, :], wx[:, g % 6, r % 2, :], ACT.Copy).then_inc(m["high"], 1)

                await_stores(act, 2 * l + 2)
                for r in range(4):
                    high(0, r)
                act.wait_ge(m["tx"], 1)
                go(xTh.rearrange("p k n -> p (k n)"), psf[:, 4 * 512:6 * 512], ACT.Copy).then_inc(m["high"], 1)
                nb = act.value_load(table[0:1, 31:32], min_val=NX, max_val=NB - 1)
                with act.Fori(0, nb) as b:
                    for r in range(4, 20):
                        high(b, r)
                    for q in range(2):
                        act.wait_ge(m["ab"], b + 1) if q == 0 else act.wait_ge(m["used"], b * 8 + 12)
                        go(s0[:, 512 * q:512 * q + 512], ps[:, 2 * q, :], ACT.Silu).then_inc(m["si"], 1)
                    for q in range(2):
                        act.wait_ge(m["tg"], b * 2 + (q + 1))
                        go(gTh[:, 4 * q:4 * q + 4, :], ps[:, q, :].rearrange("p (k n) -> p k n", n=P),
                           ACT.Copy).then_inc(m["high"], 1)
                    act.wait_ge(m["tx"], b + 2)
                    go(xTh.rearrange("p k n -> p (k n)"), psf[:, 4 * 512:6 * 512], ACT.Copy).then_inc(m["high"], 1)
                    for r in range(20, 24):
                        high(b, r)
                    for r in range(4):
                        high(b, r, 1)
                act.wait_ge(m["yst"], nb * 16 + 16)
                act.wait_ge(m["xg"], nb * 16 + 16)
                act.wait_ge(m["low"], nb * PARTS + 5)
                go(ss[:, 0:1], ones[:, 0:1], ACT.Copy).then_inc(m["done"], 1)

            act.wait_ge(s_one, 3)
            chain(0)
            act.wait_ge(par_rdy, 3)
            act.wait_ge(pad_z, 7)
            for kind, i, _ in AB_ORDER:
                if kind == "gate":
                    act.wait_ge(ab_u, i + 1)
                    if i >= 2:
                        act.wait_ge(glu_done, i - 1)
                    b0 = 1536 * (i % 2) + S
                    go(sg[i % 2], psf[:, b0:b0 + S], ACT.Sigmoid).then_inc(sg_rdy, 1)
                if kind == "pool":
                    act.wait_ge(pl_u, i + 1)
                    if i >= 2:
                        act.wait_ge(pool_s, POOL_DONE[i - 2])
                    rows = psf[:, 3072:3072 + S].rearrange("p (r w) -> p r w", w=GRID_W)
                    go(bpad[i % 2][:, :, PH:PH + GRID_W], rows[:, 0:CROWS], ACT.Copy)
                    go(lpad[i % 2][:, PH:PH + LROWS], rows[:, CROWS:], ACT.Copy).then_inc(bp_rdy, 1)
                if kind == "pooled":
                    act.wait_ge(pg_mm, i + 1)
                    go(catT[:, KD + i, :], psf[:, 3072:3072 + S], ACT.Identity,
                       scale=par[:, i, TAPS + 4:TAPS + 5], bias=pscb[:, i:i + 1]).then_inc(p_rdy, 1)
            for ct in range(KD):
                act.wait_ge(ln_d, ct + 1)
                if ct >= 2:
                    act.wait_ge(ln_sm, ct - 1)
                go(sg[ct % 2], catT[:, ct, :], ACT.Square).then_inc(ln_sq, 1)
            act.wait_ge(ln_ve, 1)
            act.wait_ge(ln_sm, KD)
            go(sg[0], lnv, ACT.Sqrt).then_inc(ln_sd, 1)
            for ct in range(KD):
                act.wait_ge(ln_n, ct + 1)
                go(catT[:, ct, :], catT[:, ct, :], ACT.Silu, scale=par[:, ct, TAPS + 1:TAPS + 2],
                   bias=par[:, ct, TAPS + 2:TAPS + 3]).then_inc(ln_y, 1)
            chain(1)
            experts(0)
            chain(2)
            def high_slice(ct):
                if ct % 4 == 0:
                    act.wait_ge(cw, 16 * (ct // 4 + 1))
                if ct >= 4:
                    act.wait_ge(xm_mm, ct - 3)
                cols = slice(ct % 4 * P, ct % 4 * P + P)
                go(cwh[:, :, cols], craw[:, :, cols], ACT.Copy).then_inc(c_high, 1)

            def high_chunks(g):
                act.wait_ge(cw, 16 * (g + 5))
                for k in range(KD):
                    if g == 0:
                        act.wait_ge(xm_mm, KE)
                    elif k < KD - 1:
                        act.wait_ge(z_use, (KD - 1) * (g - 1) + k + 1)
                    else:
                        act.wait_ge(z_mm, 4 * g)
                    go(cwh[:, k, :], craw[:, k, :], ACT.Copy).then_inc(c_high, 1)

            act.wait_ge(h_rdy, 3 * NT)
            await_stores(act, 3)
            for ct in range(4):
                high_slice(ct)
            for ct in range(KE):
                if ct + 4 < KE:
                    high_slice(ct + 4)
                act.wait_ge(cv_s, CV_OPS * (ct + 1))
                go(xc[:, ct, :], xc[:, ct, :], ACT.Silu).then_inc(xc_rdy, 1)
                if ct == KE - 4:
                    high_chunks(0)
            for z in range(16):
                g, i = z // 4, z % 4
                if i == 3 and g < 3:
                    high_chunks(g + 1)
                act.wait_ge(z_mm, z + 1)
                if z >= 2:
                    act.wait_ge(z_st[z % 2], 16 * (z // 2))
                go(zst[z % 2], ps[:, z % 8, :], ACT.Sigmoid).then_inc(z_rdy, 1)
                act.wait_ge(z_rdy, z + 1)
                act.dma_start(zs_d[i * P:(i + 1) * P, g * 512:(g + 1) * 512], zst[z % 2]).then_inc(z_st[z % 2], 16)
            for bt in range(12):
                act.wait_ge(bt_mm, bt + 1)
                if bt >= 2:
                    act.wait_ge(ge_mm, bt - 1)
                go(bdt[bt % 2], ps[:, bt % 2, :].rearrange("p (a b) -> p a b", b=P), ACT.Copy).then_inc(bt_ev, 1)
            act.wait_ge(ge_mm, 12)
            act.wait_ge(xm_z, 4)
            pg = ps[:, 2, :].rearrange("p (t a h) -> p t a h", a=4, h=H)
            gv = geff.rearrange("p t (a n) -> p t a n", a=4)
            for i in range(4):
                go(gv[:, :, i, 0:H], pg[:, :, GATE_COL[i], :], ACT.Copy).then_inc(ge_rdy, 1)
            act.wait_ge(gr, R_F)
            act.wait_ge(ge_mm, 12)
            go(r_x[0:64, :], r_lf[0:64, :], ACT.Abs).then_inc(ga, 1)
            act.wait_ge(ga, 1)
            go(r_x[0:64, :], r_x[0:64, :], ACT.Exp, scale=-1.0).then_inc(ga, 1)
            act.wait_ge(ga, 2)
            go(r_x[0:64, :], r_x[0:64, :], ACT.Ln, bias=ones[0:64, 0:1]).then_inc(ga, 1)
            act.wait_ge(gr, R_X)
            go(r_fl[0:64, :], r_x[0:64, :], ACT.Exp, scale=-1.0).then_inc(ga, 1)
            for h in range(H):
                act.wait_ge(v_mm, h + 1)
                for tt in range(0, NT, 2):
                    go(vv[h][:, tt, :], ps[:, tt, :], ACT.Copy).then_inc(v_ev, 1)
            for t in range(KE):
                act.wait_ge(kq_mm, t + 1)
                b0 = 4 * (t % 2)
                go(xc[:, t, 0:S_CTX], ps[:, b0, 256:512], ACT.Copy).then_inc(k_ev, 1)
                go(xc[:, t, S_CTX + 2:], ps[:, b0 + 1, :], ACT.Copy).then_inc(k_ev, 1)
            act.wait_ge(st_rdy, 2)
            act.wait_ge(ab_in, 16)

            def exps(u):
                h, i = u // 4, u % 4
                o = S_CTX + i * P
                if u:
                    act.wait_ge(aA, 4 * u)
                f, b = st[:, 0, i, 0, h:h + 1], st[:, 0, i, 1, h:h + 1]
                go(Ef[:, 0:o], abc[:, h, 0:o], ACT.Exp, bias=f)
                go(Eb[:, 0:S_CTX], abc[:, H + h, 0:S_CTX], ACT.Exp, bias=b)
                if i < 3:
                    go(Eb[:, o + P:S], abc[:, H + h, o + P:S], ACT.Exp, bias=b)
                act.wait_ge(dg, 2 * u + 2)
                go(Ef[:, o:o + P], Ef[:, o:o + P], ACT.Exp, bias=f)
                go(Eb[:, o:o + P], Eb[:, o:o + P], ACT.Exp, bias=b).then_inc(eE, 1)

            def y_out(u):
                act.wait_ge(yT_mm, u + 1)
                h, i = u // 4, u % 4
                go(qT[:, h * HC:(h + 1) * HC, i * P:(i + 1) * P], ps[:, 7, :].rearrange("p (a b) -> p a b", b=P),
                   ACT.Copy).then_inc(yT_ev, 1)

            exps(0)
            for u in range(16):
                act.wait_ge(tT, u + 1)
                if u:
                    act.wait_ge(pV, u)
                go(AT, psf[:, 4 * 512:4 * 512 + S], ACT.Copy).then_inc(aT, 1)
                if u:
                    y_out(u - 1)
                if u + 1 < 16:
                    exps(u + 1)
                act.wait_ge(lV, u + 1)
                go(bst[:, u % 2, 8:9], bst[:, u % 2, 7:8], ACT.Ln, bias=epsc[:]).then_inc(lX, 1)
                act.wait_ge(lX, 2 * u + 1)
                go(bst[:, u % 2, 9:10], bst[:, u % 2, 8:9], ACT.Exp, scale=-0.5).then_inc(lX, 1)
            y_out(15)
            chain(3)
            experts(1)
            chain(4)

        @block.vector
        def _(v):
            n = [0]

            def link(ins):
                n[0] += 1
                ins.then_inc(dv, 1)
                v.wait_ge(dv, n[0])

            v.memset(ones[:], 1.0).then_inc(s_one, 1)
            v.memset(onesd[:], 1.0 / D).then_inc(s_one, 1)
            v.memset(epsc[:], EPS).then_inc(s_one, 1)
            link(v.memset(gbias[:], 0.0))
            for part in (scTh, scTl):
                v.memset(part.bitcast(F32), 0.0).then_inc(s_one, 1)
            v.wait_ge(s_sc, 2)
            scv = scT.rearrange("p (v k) -> p k v", v=2)
            v.tensor_tensor(scTl[:, :, 0:2], scv, scTh[:, :, 0:2].bitcast(F32), ALU.subtract).then_inc(s_sc, 1)
            v.wait_ge(s_start, 16 * 5)

            def ada_bias(i, s):
                v.wait_ge(ada_mm, twice(i, s, 2))
                if i is None:
                    col = bada[0:2, s * 512:s * 512 + 512]
                else:
                    col = bada[0:2, bass.ds(i * 512 + s * 512, 512)]
                v.tensor_tensor(stage[s % NW][0:2, :], ps[0:2, s % NW, :], col, ALU.add).then_inc(ada_row, 1)

            for l, nn, i in ada_groups(v):
                for s in range(NW):
                    for q in range(2):
                        rows = slice(HK * q, HK * q + HK)
                        v.wait_ge(ada_high, twice(i, s, q + 1))
                        v.tensor_tensor(adal[:, s % 2, rows], adaw[:, s, rows], adah[:, s % 2, rows].bitcast(F32),
                                        ALU.subtract).then_inc(ada_low, 1)
                    if i is not None:
                        v.wait_ge(ada_st[(s - 1) % NW], 4 * i)
                        ada_bias(i, s - 1)
                    elif s:
                        ada_bias(None, s - 1)
                if i is None:
                    v.wait_ge(par_tr, 1)
                    v.tensor_copy(par[:].rearrange("p k n -> p (k n)"), ps[:, 5, 0:KD * NPAR]).then_inc(par_rdy, 1)
                    v.tensor_copy(par2[:].rearrange("p (h k) n -> p h k n", h=2),
                                  ps[:, 6, 0:5 * KE].rearrange("p (k h n) -> p h k n", h=2, n=5)).then_inc(par_rdy, 1)
                    v.wait_ge(par_rdy, 2)
                    v.tensor_tensor(pscb[:], par[:, :, TAPS + 3], par[:, :, TAPS + 4], ALU.mult).then_inc(par_rdy, 1)
            v.wait_ge(ada_st[NW - 1], 16 * 2 * NA // NW)
            v.wait_ge(ada_mm, 4 * NA)
            v.tensor_tensor(stage[NW - 1][0:2, :], ps[0:2, NW - 1, :], bada[0:2, 12 * D - 512:12 * D], ALU.add
                            ).then_inc(ada_row, 1)

            def low_input(t, j):
                v.wait_ge(ht_rdy, j + 1)
                cols = slice(t * P, (t + 1) * P)
                v.tensor_tensor(hTl[:, :, cols], psf[:, 4 * 512:6 * 512].rearrange("p (k n) -> p k n", n=P),
                                hTh[:, :, cols].bitcast(F32), ALU.subtract).then_inc(hl_rdy, 1)

            def chain(nn):
                ch = CH[nn]
                m, tmp = ch["mod"], ch["tmp"]
                v.wait_ge(s_mod, MODS[nn])
                if nn < 4:
                    for o in ((3,) if nn == 3 else (0, 3)):
                        link(v.scalar_tensor_tensor(m[o], m[o], 1.0, tmp, ALU.add, ALU.mult))
                def add(t, j):
                    s = j % 2
                    o = 0 if t < CT else 3
                    xt = ch["xt"][x_place(nn, j)]
                    v.wait_ge(xt_in[x_place(nn, j)], 16 * loads(nn, j))
                    if nn in (1, 3):
                        v.wait_ge(y_mm, y_before(nn, t) + 1)
                        b0 = 2 * s * 512
                        link(v.tensor_tensor(tmp, psf[:, b0:b0 + D], m[o + 2], ALU.mult))
                        v.tensor_tensor(xt, xt, tmp, ALU.add).then_inc(x_new, 1)
                    if nn in (2, 4):
                        v.wait_ge(y_in[s], 32 * y_gathered(nn, j))
                        ya, yb = ch["y"][0][s], ch["y"][1][s]
                        link(v.tensor_scalar(ya, ya, wsel[:, 0, t:t + 1], None, ALU.mult))
                        link(v.scalar_tensor_tensor(ya, yb, wsel[:, 1, t:t + 1], ya, ALU.mult, ALU.add))
                        link(v.tensor_tensor(ya, ya, m[o + 2], ALU.mult))
                        v.tensor_tensor(xt, xt, ya, ALU.add).then_inc(x_new, 1)

                def normed(t, j):
                    s = j % 2
                    o = 0 if t < CT else 3
                    xt = ch["xt"][x_place(nn, j)]
                    if nn:
                        v.wait_ge(x_new, j + 1 - NT)
                    v.wait_ge(rt_rdy, j + 1)
                    link(v.reciprocal(rs[:, s:s + 1], rt[:, s:s + 1]))
                    dst = hall[:, t, :] if nn in (1, 3) else ch["h"][s]
                    if nn == 4:
                        v.scalar_tensor_tensor(dst, xt, rs[:, s:s + 1], tmp, ALU.mult, ALU.mult).then_inc(h_rdy, 1)
                    else:
                        link(v.scalar_tensor_tensor(dst, xt, rs[:, s:s + 1], m[o], ALU.mult, ALU.mult))
                        v.tensor_tensor(dst, dst, m[o + 1], ALU.add).then_inc(h_rdy, 1)

                tl = tiles_of(nn)
                if nn in (2, 4):
                    add(*tl[0])
                for i, (t, j) in enumerate(tl):
                    if nn not in (2, 4):
                        add(t, j)
                    elif i + 1 < len(tl):
                        add(*tl[i + 1])
                    normed(t, j)
                    if nn == 2 and t:
                        low_input(t - 1, j - 1)
                if nn == 2:
                    low_input(t, j)

            def router(l):
                t0 = 0 if l == 0 else CT
                T = NT - t0

                def tv(a):
                    return a[:, t0:, :]

                def tf(a):
                    return tv(a).rearrange("p t e -> p (t e)")

                def tg(a):
                    return tf(a).rearrange("p (g e) -> p g e", e=4)

                TG = T * 4
                v.wait_ge(sc_rdy, l + 1)
                link(v.tensor_tensor(tv(r_bi), tv(r_sc), bc(brow[:], 1, T), ALU.add))
                tie = bc(cst[:, C_TIE:C_TIE + 16].rearrange("p (i j) -> p i j", j=4), 1, TG)

                def rank(dst, a, n_, tie_):
                    x1 = r_big[:, 0:n_ * 16].rearrange("p (g i j) -> p g i j", i=4, j=4)
                    x2 = r_big2[:, 0:n_ * 16].rearrange("p (g i j) -> p g i j", i=4, j=4)
                    v.tensor_tensor(x1, bc(a, 2, 4), bc(a, 3, 4), ALU.is_gt)
                    link(v.tensor_tensor(x2, bc(a, 2, 4), bc(a, 3, 4), ALU.is_equal))
                    link(v.tensor_tensor(x2, x2, tie_, ALU.mult))
                    link(v.tensor_tensor(x1, x1, x2, ALU.add))
                    link(v.tensor_reduce(dst, x1, AX.X, ALU.add))

                rank(tg(r_t), tg(r_bi), TG, tie)
                link(v.tensor_scalar(tf(r_t), tf(r_t), 2.0, None, ALU.is_lt))
                link(v.tensor_tensor(tf(r_f), tf(r_bi), tf(r_t), ALU.mult))
                gs = r_s[:, 0:TG]
                link(v.tensor_reduce(gs, tg(r_f), AX.X, ALU.add))
                gr_ = r_s[:, 24:24 + TG]
                rank(gr_.rearrange("p (t g) -> p t g", g=4), gs.rearrange("p (t g) -> p t g", g=4), T,
                     bc(cst[:, C_TIE:C_TIE + 16].rearrange("p (i j) -> p i j", j=4), 1, T))
                link(v.tensor_scalar(gr_, gr_, 1.0, None, ALU.is_lt))
                v.tensor_tensor(tg(r_m), tg(r_t), bc(gr_, 2, 4), ALU.mult).then_inc(mk_rdy, 1)
                v.wait_ge(mk_rdy, l + 1)
                link(v.tensor_tensor(tf(r_w), tf(r_sc), tf(r_m), ALU.mult))
                sw = r_s[:, 48:48 + T]
                link(v.tensor_reduce(sw, tv(r_w), AX.X, ALU.add))
                link(v.reciprocal(sw, sw))
                link(v.tensor_tensor(tv(r_w), tv(r_w), bc(sw, 2, NX), ALU.mult))
                v.wait_ge(pos_rdy, l + 1)
                link(v.tensor_copy(tf(r_pos), ps[:, 7, t0 * NX:NT * NX]))
                cnt = r_s[:, 56:72]
                link(v.tensor_reduce(cnt, ps[:, 7, P:P + T * NX].rearrange("p (t e) -> p e t", e=NX), AX.X, ALU.add))
                th = cst[:, C_TH:C_TH + FMAX]
                big = r_big[:, 0:NX * FMAX].rearrange("p (e f) -> p e f", f=FMAX)
                link(v.tensor_tensor(big, bc(cnt, 2, FMAX), bc(th, 1, NX), ALU.is_gt))
                ov, cum, ovs = r_s[:, 72:88], r_s[:, 88:104], r_s[:, 104:120]
                link(v.tensor_reduce(ov, big, AX.X, ALU.add))
                link(v.tensor_tensor_scan(cum, ones[:, 0:NX], ov, 0.0, ALU.mult, ALU.add))
                link(v.tensor_tensor(ovs, cum, ov, ALU.subtract))
                big = r_big[:, 0:T * NX * FMAX].rearrange("p (e f) -> p e f", f=FMAX)
                link(v.tensor_tensor(big, bc(tf(r_pos), 2, FMAX), bc(th, 1, T * NX), ALU.is_ge))
                link(v.tensor_reduce(tf(r_f), big, AX.X, ALU.add))
                e_row = cst[:, C_E:C_E + NX]
                d_ = r_s[:, 120:136]
                link(v.scalar_tensor_tensor(d_, ovs, NX - 1.0, e_row, ALU.add, ALU.subtract))
                link(v.tensor_tensor(tv(r_sl), tv(r_f), bc(d_, 1, T), ALU.add))
                link(v.tensor_scalar(tf(r_t), tf(r_f), 1.0, None, ALU.min))
                link(v.tensor_tensor(tf(r_sl), tf(r_sl), tf(r_t), ALU.mult))
                link(v.tensor_tensor(tv(r_sl), tv(r_sl), bc(e_row, 1, T), ALU.add))
                link(v.scalar_tensor_tensor(tf(r_pos), tf(r_f), -float(P), tf(r_pos), ALU.mult, ALU.add))
                link(v.scalar_tensor_tensor(tf(r_sl), tf(r_pos), float(NB), tf(r_sl), ALU.mult, ALU.add))
                link(v.scalar_tensor_tensor(tf(r_sl), tf(r_sl), 1.0, tf(r_m), ALU.add, ALU.mult))
                link(v.tensor_scalar(tf(r_t), tf(r_m), -BIG, BIG, ALU.mult, ALU.add))
                link(v.tensor_tensor(tf(r_t), tf(r_t), tf(r_sl), ALU.add))
                sk = r_s[:, 136:136 + 2 * NT].rearrange("p (k t) -> p k t", k=2)
                link(v.tensor_reduce(sk[:, 0, t0:], tv(r_sl), AX.X, ALU.max))
                link(v.tensor_reduce(sk[:, 1, t0:], tv(r_t), AX.X, ALU.min))
                for k in range(2):
                    link(v.tensor_tensor(tv(r_f), tv(r_sl), bc(sk[:, k, t0:], 2, NX), ALU.is_equal))
                    link(v.tensor_tensor(tf(r_f), tf(r_f), tf(r_w), ALU.mult))
                    link(v.tensor_reduce(wsel[:, k, t0:], tv(r_f), AX.X, ALU.add))
                link(v.tensor_scalar(slots[:, :, t0:], sk[:, :, t0:], -1.0, None, ALU.add))
                tb = r_s[0:1, 160:192]
                j_row = cst[0:1, C_J:C_J + NB - NX]
                tbig = r_big[0:1, 0:(NB - NX) * NX].rearrange("p (j e) -> p j e", e=NX)
                link(v.tensor_tensor(tbig, bc(cum[0:1, :], 1, NB - NX), bc(j_row, 2, NX), ALU.is_le))
                link(v.memset(tb, 0.0))
                link(v.tensor_reduce(tb[:, NX:NB], tbig, AX.X, ALU.add))
                link(v.tensor_scalar(tb[:, NX:NB], tb[:, NX:NB], NX - 1.0, None, ALU.min))
                link(v.tensor_copy(tb[:, 0:NX], e_row[0:1, :]))
                link(v.tensor_scalar(tb[:, 31:32], cum[0:1, NX - 1:NX], float(NX), None, ALU.add))
                v.tensor_copy(table[:], tb).then_inc(sl_rdy, 1)

            def experts(l):
                m = moe[l]

                def low(b, r, ahead=0, first=False):
                    v.wait_ge(m["high"], r + 1 if first else made(b, "chunk", r, PARTS * ahead))
                    v.tensor_tensor(wl[:, r % NHL, :], wx[:, r // 2 % 6, r % 2, :], wh[:, r % NHL, :].bitcast(F32),
                                    ALU.subtract).then_inc(m["low"], 1)

                def low_x():
                    v.tensor_tensor(xTl.rearrange("p k n -> p (k n)"), psf[:, 4 * 512:6 * 512],
                                    xTh.rearrange("p k n -> p (k n)").bitcast(F32), ALU.subtract).then_inc(m["low"], 1)

                for r in range(4):
                    low(None, r, first=True)
                v.wait_ge(m["high"], 5)
                low_x()
                v.memset(yy, 0.0).then_inc(m["ye"], 1)
                nb = v.value_load(table[0:1, 31:32], min_val=NX, max_val=NB - 1)
                with v.Fori(0, nb) as b:
                    for r in range(4, 20):
                        low(b, r)
                    for q in range(2):
                        v.wait_ge(m["si"], b * 2 + (q + 1))
                        v.tensor_tensor(gg[:, 512 * q:512 * q + 512], s0[:, 512 * q:512 * q + 512],
                                        ps[:, 2 * q + 1, :], ALU.mult).then_inc(m["g"], 1)
                    for q in range(2):
                        v.wait_ge(m["high"], made(b, "g", q))
                        v.tensor_tensor(gTl[:, 4 * q:4 * q + 4, :], ps[:, q, :].rearrange("p (k n) -> p k n", n=P),
                                        gTh[:, 4 * q:4 * q + 4, :].bitcast(F32), ALU.subtract).then_inc(m["low"], 1)
                    v.wait_ge(m["high"], made(b, "x", 0, PARTS - 4))
                    low_x()
                    for r in range(20, 24):
                        low(b, r)
                    for r in range(4):
                        low(b, r, 1)
                    v.wait_ge(m["used"], b * 8 + 16)
                    v.wait_ge(m["yst"], b * 16 + 16)
                    v.tensor_copy(yy, psf[:, 6 * 512:8 * 512]).then_inc(m["ye"], 1)

            chain(0)
            v.wait_ge(pad_z, 7)
            for ct in range(KD):
                ap = apad[ct % 2]
                b0 = 3 * (ct % 2)
                v.wait_ge(sg_rdy, ct + 1)
                if ct:
                    v.wait_ge(conv_s, CONV_OPS * ct)
                v.tensor_tensor(ap[:, :, HALO:HALO + GRID_W], psf[:, b0 * 512:b0 * 512 + S].rearrange("p (r w) -> p r w", w=GRID_W),
                                sg[ct % 2].rearrange("p (r w) -> p r w", w=GRID_W), ALU.mult).then_inc(glu_done, 1)
                v.wait_ge(glu_done, ct + 1)
                v.tensor_copy(ap[:, 0:CROWS - 1, HALO + GRID_W:RW], ap[:, 1:CROWS, HALO:2 * HALO]).then_inc(conv_s, 1)
                v.tensor_copy(ap[:, 1:CROWS, 0:HALO], ap[:, 0:CROWS - 1, GRID_W:GRID_W + HALO]).then_inc(conv_s, 1)
                acc = [catT[:, ct, :].rearrange("p (r w) -> p r w", w=GRID_W), acc1.rearrange("p (r w) -> p r w", w=GRID_W)]
                for k in range(TAPS):
                    src, w = ap[:, :, k:k + GRID_W], par[:, ct, k:k + 1]
                    v.wait_ge(conv_s, CONV_OPS * ct + (2 if k < 2 else k + 1))
                    if k == 0:
                        ins = v.tensor_scalar(acc[0], src, w, par[:, ct, TAPS:TAPS + 1], ALU.mult, ALU.add)
                    elif k == 1:
                        ins = v.tensor_scalar(acc[1], src, w, None, ALU.mult)
                    else:
                        ins = v.scalar_tensor_tensor(acc[k % 2], src, w, acc[k % 2], ALU.mult, ALU.add)
                    ins.then_inc(conv_s, 1)
                v.wait_ge(conv_s, CONV_OPS * ct + 2 + TAPS)
                v.tensor_tensor(acc[0], acc[0], acc[1], ALU.add).then_inc(conv_s, 1)
            v.wait_ge(ln_mu, 1)
            for ct in range(KD):
                v.tensor_tensor(catT[:, ct, :], catT[:, ct, :], psf[:, 0:S], ALU.subtract).then_inc(ln_d, 1)
            v.wait_ge(ln_sm, KD)
            v.tensor_scalar(lnv, psf[:, 2 * 512:2 * 512 + S], EPS, None, ALU.add).then_inc(ln_ve, 1)
            v.wait_ge(ln_sd, 1)
            link(v.reciprocal(sg[1], sg[0]))
            for ct in range(KD):
                v.tensor_tensor(catT[:, ct, :], catT[:, ct, :], sg[1], ALU.mult).then_inc(ln_n, 1)
            chain(1)
            router(0)
            experts(0)
            chain(2)
            def low(n, what):
                v.wait_ge(c_high, n + 1)
                v.tensor_tensor(cwl[what], craw[what], cwh[what].bitcast(F32), ALU.subtract).then_inc(c_low, 1)

            def low_slice(ct):
                low(ct, (slice(None), slice(None), slice(ct % 4 * P, ct % 4 * P + P)))

            for ct in range(4):
                low_slice(ct)
            v.wait_ge(xm_z, 3)
            for ct in range(KE):
                if ct + 4 < KE:
                    low_slice(ct + 4)
                b0 = 2 * (ct % 4) * 512
                v.wait_ge(xm_mm, ct + 1)
                v.tensor_copy(xm[:, ct, 2:2 + S_CTX], psf[:, b0:b0 + S_CTX]).then_inc(cv_s, 1)
                v.tensor_copy(xm[:, ct, 4 + S_CTX:4 + S], psf[:, b0 + S_CTX:b0 + S]).then_inc(cv_s, 1)
                for k in range(4):
                    src = xm[:, ct, k:k + XC]
                    v.wait_ge(cv_s, CV_OPS * ct + 2 + k)
                    if k == 0:
                        ins = v.tensor_scalar(xc[:, ct, :], src, par2[:, ct, 0:1], par2[:, ct, 4:5], ALU.mult, ALU.add)
                    else:
                        ins = v.scalar_tensor_tensor(xc[:, ct, :], src, par2[:, ct, k:k + 1], xc[:, ct, :], ALU.mult, ALU.add)
                    ins.then_inc(cv_s, 1)
            for i in range(4 * KD):
                low(KE + i, (slice(None), i % KD, slice(None)))
            v.wait_ge(z_mm, 16)
            v.memset(geff, 0.0).then_inc(xm_z, 1)
            g_n = [0]

            def row(ins):
                g_n[0] += 1
                ins.then_inc(gr, 1)
                v.wait_ge(gr, g_n[0])

            v.wait_ge(raw_in, 48 + 64)
            v.wait_ge(g_mm, 1)
            row(v.tensor_scalar(G, psf[:, 4 * 512 + 256:6 * 512], gbias[:], None, ALU.add))
            assert g_n[0] == R_G
            row(v.tensor_copy(r_lf[0:64, :], G[64:128, :]))
            assert g_n[0] == R_F
            row(v.memset(r_zero[0:64, :], 0.0))
            v.wait_ge(ga, 3)
            row(v.scalar_tensor_tensor(r_lf[0:64, :], r_lf[0:64, :], 0.0, r_x[0:64, :], ALU.min, ALU.subtract))
            row(v.memset(r_x[0:64, :], 1.0))

            def back(a, lo, hi):
                return a[32:36, lo:hi][:, ::-1]

            def scans(dst, d0, d1, op0, op1):
                row(v.tensor_tensor_scan(dst[0:4, :], d0[0:4, :], d1[0:4, :], 0.0, op0, op1))
                row(v.tensor_tensor_scan(back(dst, 0, S_CTX), back(d0, 0, S_CTX), back(d1, 0, S_CTX), 0.0, op0, op1))
                row(v.tensor_tensor_scan(back(dst, S_CTX, S), back(d0, S_CTX, S), back(d1, S_CTX, S),
                                         dst[32:36, 0:1], op0, op1))

            row(v.memset(r_b[0:64, :], 0.0))
            scans(r_b, r_x, r_lf, ALU.mult, ALU.add)
            row(v.tensor_tensor(r_a[0:64, :], G[0:64, :], r_b[0:64, :], ALU.subtract))
            assert g_n[0] == R_A, g_n
            row(v.memset(r_M[0:64, :], 0.0))
            scans(r_M, r_zero, r_a, ALU.add, ALU.max)
            row(v.tensor_tensor(r_x[0:64, :], r_b[0:64, :], r_M[0:64, :], ALU.add))
            assert g_n[0] == R_X, g_n
            row(v.tensor_scalar(r_M[0:64, :], r_M[0:64, :], -1.0, None, ALU.mult))
            assert g_n[0] == R_M, g_n
            for h in range(H):
                v.wait_ge(v_mm, h + 1)
                for tt in range(1, NT, 2):
                    v.tensor_copy(vv[h][:, tt, :], ps[:, tt, :]).then_inc(v_ev, 1)
            v.wait_ge(stt_mm, 1)
            for kind in range(2):
                v.tensor_copy(st[:, kind], ps[:, 6 + kind, 0:256].rearrange("p (i d r) -> p i d r", i=4, d=2)[:, :, :, 0:H]
                              ).then_inc(st_rdy, 1)
            v.wait_ge(ar_st, 32)
            for t in range(KE):
                v.wait_ge(kq_mm, t + 1)
                v.tensor_copy(qT[:, t, :], ps[:, 4 * (t % 2) + 2, :]).then_inc(q_ev, 1)
            scale = DH ** -0.5

            def weigh(u):
                h, i = u // 4, u % 4
                o = S_CTX + i * P
                sc_ = psf[:, 2 * (u % 2) * 512 + 256:2 * (u % 2) * 512 + 1024]
                d = dn[:, u % 2]
                A = AA[u % 2]
                v.wait_ge(sS, u + 1)
                v.wait_ge(eE, u + 1)
                if u >= 2:
                    v.wait_ge(tT, u - 1)
                v.scalar_tensor_tensor(Ef[:, 0:o + P], sc_[:, 0:o + P], scale, Ef[:, 0:o + P], ALU.mult, ALU.mult,
                                       accum_out=d[:, 0:1])
                v.scalar_tensor_tensor(Eb[:, 0:S_CTX], sc_[:, 0:S_CTX], scale, Eb[:, 0:S_CTX], ALU.mult, ALU.mult,
                                       accum_out=d[:, 1:2])
                v.scalar_tensor_tensor(Eb[:, o:S], sc_[:, o:S], scale, Eb[:, o:S], ALU.mult, ALU.mult,
                                       accum_out=d[:, 2:3]).then_inc(aA, 1)
                v.wait_ge(aA, 4 * u + 1)
                link(v.tensor_tensor(d[:, 1:2], d[:, 1:2], d[:, 2:3], ALU.add))
                link(v.scalar_tensor_tensor(d[:, 4:6], d[:, 0:2], -1.0, d[:, 0:2], ALU.mult, ALU.max))
                link(v.tensor_tensor(d[:, 4:6], d[:, 4:6], st[:, 1, i, :, h], ALU.max))
                link(v.reciprocal(d[:, 6:8], d[:, 4:6]))
                v.tensor_scalar(A[:, 0:o + P], Ef[:, 0:o + P], d[:, 6:7], None, ALU.mult).then_inc(aA, 1)
                v.wait_ge(aA, 4 * u + 2)
                if i < 3:
                    v.tensor_scalar(A[:, o + P:S], Eb[:, o + P:S], d[:, 7:8], None, ALU.mult)
                v.scalar_tensor_tensor(A[:, 0:S_CTX], Eb[:, 0:S_CTX], d[:, 7:8], A[:, 0:S_CTX], ALU.mult, ALU.add
                                       ).then_inc(aA, 1)
                v.scalar_tensor_tensor(A[:, o:o + P], Eb[:, o:o + P], d[:, 7:8], A[:, o:o + P], ALU.mult, ALU.add
                                       ).then_inc(aA, 1)

            def head_norm(u):
                h, i = u // 4, u % 4
                bs = bst[:, u % 2]
                v.wait_ge(pV, u + 1)
                link(v.bn_stats(bs[:, 0:6], ps[:, 6, :]))
                v.bn_aggr(bs[:, 6:8], bs[:, 0:6]).then_inc(lV, 1)
                v.wait_ge(lX, 2 * u + 2)
                if u:
                    v.wait_ge(yT_mm, u)
                link(v.tensor_scalar(hv, ps[:, 6, :], bs[:, 6:7], bs[:, 9:10], ALU.subtract, ALU.mult))
                v.wait_ge(hn_in, 16 * (h + 1))
                link(v.tensor_tensor(hv, hv, hn, ALU.mult))
                v.wait_ge(zl_in[u % 2], 16 * (u // 2 + 1))
                v.tensor_tensor(hv, hv, zl[u % 2], ALU.mult).then_inc(hV, 1)

            for s in range(2):
                v.wait_ge(z_st[s], 16 * 8)
            weigh(0)
            for u in range(16):
                if u + 1 < 16:
                    weigh(u + 1)
                head_norm(u)
            chain(3)
            router(1)
            experts(1)
            chain(4)


def x_place(n, j):
    return (j - tiles_of(n)[0][1]) % 3 if n in (2, 4) else j % 2


def lg_before(n, t):
    return t if n == 1 else NT + t - CT


def y_before(n, t):
    return lg_before(n, t)


def made(b, what, i, shift=0):
    n = {"x": 1, "chunk": i + 2 if i < 20 else i + 5, "g": 22 + i}[what] + shift
    return n if b is None else b * PARTS + n


def y_gathered(n, j):
    return sum(1 for m, t, i in CHAINS if m in (2, 4) and i <= j and i % 2 == j % 2)


AR = 51200
NW = 4
HK = KD // 2
PARTS = 3 * KD + 3
NHL = 8
CONV_OPS = 2 + TAPS + 1
CV_OPS = 6
GATE_COL = (0, 2, 1, 3)
R_G, R_F, R_A, R_X, R_M = 1, 2, 10, 15, 16
A_FL = 4
POOL_DONE = []
for _p in range(KD):
    POOL_DONE.append((POOL_DONE[-1] if _p else 0) + 2 + 2 * (_p // 2 + 1) + 4)
AB_ORDER, _last = [], None
for _s in range(4 * KD):
    _todo = [(("value", "gate")[_s % 2], _s // 2)] if _s < 2 * KD else []
    if _s % 2 == 0 and _s < 2 * KD:
        _todo.append(("pool", _s // 2))
    if _s % 2 == 1 and 5 <= _s < 2 * KD + 5:
        _todo.append(("pooled", (_s - 5) // 2))
    for _kind, _i in _todo:
        AB_ORDER.append((_kind, _i, _last))
        if _kind in ("pool", "pooled"):
            _last = (_kind, _i)
BATCH = [[(m_, t + i) for m_ in (0, 1) for i in range(2)] for t in range(0, KE, 2)] + \
        [[(2, t + i) for i in range(4)] for t in range(0, KE, 4)]

_INS = ['x', 'c', 'ctx', 'c_ctx', 'w_ada', 'b_ada', 'g_mix', 'g_ffn', 'g_final', 'w_in_ab', 'w_dw_a', 'b_dw_a', 'ln_g_a',
        'ln_b_a', 'w_pool', 'b_pool', 'pool_scale', 'w_out_ab', 'w_in_c', 'w_conv_c', 'b_conv_c', 'w_q', 'w_k', 'w_v',
        'w_gates', 'b_gates', 'hn_g', 'w_out_c', 'w_router', 'b_router', 'w1', 'w3', 'w2']


def kernel(**inputs):
    import numpy as _np
    import concourse.bacc as _bacc
    from concourse import mybir as _mybir
    from concourse.bass_utils import run_bass_kernel_spmd as _run

    nc = _bacc.Bacc("TRN2", target_bir_lowering=False, num_devices=1)
    arrays, args = {}, []
    consts, rcounts = constants()
    for name in _INS + ["consts", "rcounts"]:
        a = _np.ascontiguousarray({"consts": consts, "rcounts": rcounts}[name] if name in ("consts", "rcounts") else inputs[name])
        arrays[f"in_{name}_dram"] = a
        args.append(nc.dram_tensor(f"in_{name}_dram", a.shape, _mybir.dt.from_np(a.dtype), kind="ExternalInput").ap())
    args.append(nc.dram_tensor("out_0_dram", (1, S_LAT, D), _mybir.dt.float32, kind="ExternalOutput").ap())
    program(nc, *args)
    r = _run(nc, [arrays], core_ids=[0])
    return r.results[0]["out_0_dram"]
```
